# Optimizing a Trainium2 kernel written in Bass

```python
import math
import jax, jax.numpy as jnp
from jax import lax
import numpy as np

D_MODEL = 2048
BATCH = 1
SEQ = 256
DEPTH = 2

N_MIXERS = 2
POOL_WINDOWS = (2, 4, 8, 16)
N_POOL_GROUPS = len(POOL_WINDOWS)
POOL_GROUP = D_MODEL // N_POOL_GROUPS
RET_HEADS = 8
RET_QK_DIM = D_MODEL
RET_V_DIM = 2 * D_MODEL
RET_HEAD_QK = RET_QK_DIM // RET_HEADS
RET_HEAD_V = RET_V_DIM // RET_HEADS
RET_CHUNK = 128
ROPE_BASE = 10000.0
D_FF = 4 * D_MODEL
N_POOL_LAYERS = (DEPTH + 1) // 2
N_RET_LAYERS = DEPTH // 2
EPS = 1e-6
ADA_SCALE = 0.5

kernel_name = 'hybrid_pool_retention_adaln_trunk'

def rmsnorm(x, g):
    xf = x.astype(jnp.float32)
    y = xf * lax.rsqrt(jnp.mean(xf * xf, axis=-1, keepdims=True) + EPS)
    return (y * g.astype(jnp.float32)).astype(x.dtype)

def modulate(h, shift, scale):
    return h * (1 + scale[:, None, :]) + shift[:, None, :]

def pool_mixer(h, w_grp, ls):
    B, S, D = h.shape
    hf = h.astype(jnp.float32)
    cs = jnp.concatenate([jnp.zeros((B, 1, D), jnp.float32), jnp.cumsum(hf, axis=1)], axis=1)
    t = jnp.arange(S)
    outs = []
    for gi, w in enumerate(POOL_WINDOWS):
        lo_c, hi_c = gi * POOL_GROUP, (gi + 1) * POOL_GROUP
        cs_g = cs[:, :, lo_c:hi_c]
        lo = jnp.maximum(t + 1 - w, 0)
        cnt = (t + 1 - lo).astype(jnp.float32)
        mean = (cs_g[:, 1:] - cs_g[:, lo]) / cnt[None, :, None]
        outs.append(mean - hf[:, :, lo_c:hi_c])
    p = jnp.stack(outs, axis=2).astype(h.dtype)
    y = jnp.einsum('bsgc,gcd->bsgd', p, w_grp).reshape(B, S, D)
    return y * ls

def rotary(x, pos):
    d = x.shape[-1]
    inv = ROPE_BASE ** (-jnp.arange(0, d, 2, dtype=jnp.float32) / d)
    ang = pos.astype(jnp.float32)[:, None] * inv[None, :]
    cos = jnp.cos(ang)[None, :, None, :]
    sin = jnp.sin(ang)[None, :, None, :]
    x1, x2 = x[..., 0::2], x[..., 1::2]
    return jnp.stack([x1 * cos - x2 * sin, x1 * sin + x2 * cos], axis=-1).reshape(x.shape)

def retention(h, w_in, w_out):
    B, S, _ = h.shape
    H, dk, dv, C = RET_HEADS, RET_HEAD_QK, RET_HEAD_V, RET_CHUNK
    n = S // C
    proj = h @ w_in
    q, k, v, g = jnp.split(proj, [RET_QK_DIM, 2 * RET_QK_DIM, 2 * RET_QK_DIM + RET_V_DIM], axis=-1)
    pos = jnp.arange(S)
    q = rotary(q.reshape(B, S, H, dk).astype(jnp.float32), pos)
    k = rotary(k.reshape(B, S, H, dk).astype(jnp.float32), pos) * (dk ** -0.5)
    v = v.reshape(B, S, H, dv).astype(jnp.float32)

    gamma = 1.0 - 2.0 ** (-5.0 - jnp.arange(H, dtype=jnp.float32))
    log_g = jnp.log(gamma)
    j = jnp.arange(C, dtype=jnp.float32)
    diff = j[:, None] - j[None, :]
    intra = jnp.where(diff[None] >= 0, jnp.exp(jnp.maximum(diff, 0.0)[None] * log_g[:, None, None]), 0.0)
    q_dec = jnp.exp((j[None, :] + 1.0) * log_g[:, None])[None, :, :, None]
    k_dec = jnp.exp((C - 1.0 - j[None, :]) * log_g[:, None])[None, :, :, None]
    chunk_dec = jnp.exp(C * log_g)[None, :, None, None]

    def to_chunks(a):
        return a.reshape(B, n, C, H, a.shape[-1]).transpose(1, 0, 3, 2, 4)

    def step(state, inp):
        qc, kc, vc = inp
        scores = jnp.einsum('bhid,bhjd->bhij', qc, kc) * intra[None]
        inner = jnp.einsum('bhij,bhje->bhie', scores, vc)
        cross = jnp.einsum('bhid,bhde->bhie', qc * q_dec, state)
        new_state = chunk_dec * state + jnp.einsum('bhjd,bhje->bhde', kc * k_dec, vc)
        return new_state, inner + cross

    state0 = jnp.zeros((B, H, dk, dv), jnp.float32)
    _, y = lax.scan(step, state0, (to_chunks(q), to_chunks(k), to_chunks(v)))
    y = y.transpose(1, 0, 3, 2, 4).reshape(B, S, H, dv)
    mu = jnp.mean(y, axis=-1, keepdims=True)
    var = jnp.mean((y - mu) ** 2, axis=-1, keepdims=True)
    y = ((y - mu) * lax.rsqrt(var + EPS)).reshape(B, S, RET_V_DIM).astype(h.dtype)
    return (jax.nn.silu(g) * y) @ w_out

def sq_relu_mlp(h, w1, w2):
    a = jax.nn.relu(h @ w1)
    return (a * a) @ w2

def setup_inputs(seed: int = 0) -> dict:
    key = jax.random.key(seed)
    ks = jax.random.split(key, 13)
    D = D_MODEL
    nrm = jax.random.normal
    x = nrm(ks[0], (BATCH, SEQ, D), jnp.float32)
    c = nrm(ks[1], (BATCH, D), jnp.float32)
    ada_w = nrm(ks[2], (DEPTH, 2, D, 3 * D), jnp.float32) * (ADA_SCALE * D ** -0.5)
    ada_b = nrm(ks[3], (DEPTH, 2, 3 * D), jnp.float32) * 0.02
    norm_g = 1.0 + 0.05 * nrm(ks[4], (DEPTH, 2, D), jnp.float32)
    pool_w = nrm(ks[5], (N_POOL_LAYERS, N_POOL_GROUPS, POOL_GROUP, POOL_GROUP), jnp.float32) * POOL_GROUP ** -0.5
    pool_scale = 1.0 + 0.1 * nrm(ks[6], (N_POOL_LAYERS, D), jnp.float32)
    ret_w_in = nrm(ks[7], (N_RET_LAYERS, D, 2 * RET_QK_DIM + 2 * RET_V_DIM), jnp.float32) * D ** -0.5
    ret_w_out = nrm(ks[8], (N_RET_LAYERS, RET_V_DIM, D), jnp.float32) * RET_V_DIM ** -0.5
    mlp_w1 = nrm(ks[9], (DEPTH, D, D_FF), jnp.float32) * D ** -0.5
    mlp_w2 = nrm(ks[10], (DEPTH, D_FF, D), jnp.float32) * D_FF ** -0.5
    final_g = 1.0 + 0.05 * nrm(ks[11], (D,), jnp.float32)
    return {'x': x, 'c': c, 'ada_w': ada_w, 'ada_b': ada_b, 'norm_g': norm_g,
            'pool_w': pool_w, 'pool_scale': pool_scale, 'ret_w_in': ret_w_in, 'ret_w_out': ret_w_out,
            'mlp_w1': mlp_w1, 'mlp_w2': mlp_w2, 'final_g': final_g}

def reference(x, c, ada_w, ada_b, norm_g, pool_w, pool_scale, ret_w_in, ret_w_out, mlp_w1, mlp_w2, final_g):
    cond = jax.nn.silu(c)
    for i in range(DEPTH):
        mod = jnp.einsum('bd,sdk->bsk', cond, ada_w[i]) + ada_b[i]
        shift_t, scale_t, gate_t = jnp.split(mod[:, 0], 3, axis=-1)
        shift_m, scale_m, gate_m = jnp.split(mod[:, 1], 3, axis=-1)
        h = modulate(rmsnorm(x, norm_g[i, 0]), shift_t, scale_t)
        if i % N_MIXERS == 0:
            y = pool_mixer(h, pool_w[i // N_MIXERS], pool_scale[i // N_MIXERS])
        else:
            y = retention(h, ret_w_in[i // N_MIXERS], ret_w_out[i // N_MIXERS])
        x = x + gate_t[:, None, :] * y
        h = modulate(rmsnorm(x, norm_g[i, 1]), shift_m, scale_m)
        x = x + gate_m[:, None, :] * sq_relu_mlp(h, mlp_w1[i], mlp_w2[i])
    return rmsnorm(x, final_g)


_drawn_inputs = setup_inputs


def setup_inputs(seed=0):
    import zlib

    import numpy as np

    out = dict(_drawn_inputs(seed))
    spreads = {}
    factors = {}
    for name, (base, spread) in spreads.items():
        noise = np.random.default_rng([zlib.crc32(name.encode()), seed]).standard_normal(out[name].shape)
        drawn = base * np.exp(spread * noise) if base else spread * noise
        out[name] = __import__('jax').numpy.asarray(drawn.astype(out[name].dtype))
    for name, factor in factors.items():
        out[name] = (out[name] * factor).astype(out[name].dtype)
    return out
```

```python
from contextlib import ExitStack

import numpy as np

import concourse.bass as bass
from concourse import mybir

ALU = mybir.AluOpType
ACT = mybir.ActivationFunctionType
AX_X = mybir.AxisListType.X
F32 = mybir.dt.float32
F32R = mybir.dt.float32r

P = 128
D = 2048
S = 256
TT = S // P
KT = D // P
FF = 4 * D
NB = 512
CH = 8
CK = KT // CH
RING = 4
LEAD = RING
AW = 1024
SEG = KT * D // AW
HEADS = 8
GROUP_HEADS = 4
DV = 512
EPS = 1e-6
WINDOWS = (2, 4, 8, 16)
M_UNITS = 8
R_UNITS = 16

UNIT = {
    "m1": dict(U=1, E=1, SQ=1),
    "m2": dict(U=1, E=1, XA=1),
    "q": dict(U=1, E=1, RO=1),
    "k": dict(U=1, E=1, RO=1),
    "g": dict(U=1, E=1),
    "v": dict(U=1, E=1),
}


class Count:

    NAMES = ("U", "E", "SQ", "XA", "RO", "TB", "TL", "SC", "Y", "AD", "SG", "CS", "GB", "NO", "HT", "SB")

    def __init__(self):
        self.n = {k: 0 for k in self.NAMES}
        self.reg, self.per = None, {}

    def add(self, **more):
        for k, v in more.items():
            self.n[k] += v

    def unit(self, kind):
        self.add(**UNIT[kind])

    def of(self, k):
        per = self.per.get(k, 0)
        return self.n[k] if self.reg is None or per == 0 else self.reg * per + self.n[k]

    def enter(self, reg, per):
        self.reg, self.per, self.kept = reg, per, dict(self.n)

    def leave(self, trips):
        for k in self.NAMES:
            seen = self.n[k] - self.kept[k]
            assert seen <= self.per.get(k, 0), (k, seen, self.per)
            self.n[k] = self.kept[k] + trips * self.per.get(k, 0)
        self.reg, self.per = None, {}


M_KINDS = ["m1"] * 4 + ["m2"] * 4
PAIR = ["q", "k", "g", "v", "g", "v"]
R_KINDS = PAIR * 2 + ["m2"] * 4

ADA_GATE_NOW = ([8, 6, 6, 6, 6, 0, 0, 0], "now")
ADA_COL = ([4] * 8, "col")
ADA_GATE_KEPT = ([5, 5, 5, 5, 4, 4, 4, 0], "kept")
ADA_NONE = ([0] * 8, None)
M_ROUND = dict(U=8, E=8, SQ=4, XA=4, TB=8, TL=8, SB=3)
R_ROUND = dict(U=16, E=20, XA=4, RO=4, TB=16, TL=8, SC=4, Y=4, AD=SEG, SG=1, CS=1, SB=3)


def mlp_round(plan):
    spread, what = plan
    return dict(M_ROUND, AD=sum(spread), SG=1 if what else 0, CS=1 if what == "col" else 0)


MLP_PLAN = {
    0: [(0, 1, ADA_GATE_NOW), (1, 2, ADA_COL), (3, 1, ADA_GATE_KEPT)],
    1: [(0, 1, ADA_GATE_NOW), (1, 2, ADA_NONE), (3, 1, ADA_NONE)],
}

PE_STEPS = {1: {4: ["T rot"]}, 2: {3: ["T rot"]}, 3: {1: [("scores", 0)]}, 4: {3: [("weigh", 0)]},
            5: {1: [("scores", 1)], 3: ["T z"]},
            6: {3: [("weigh", 1)]}, 7: {2: ["T z"], 4: ["T rot"]}, 8: {3: ["T rot"]},
            9: {1: [("scores", 2)]}, 10: {3: [("weigh", 2)]}, 11: {1: [("scores", 3)], 3: ["T z"]},
            12: {0: [("weigh", 3)], 3: ["T z"]}}
ACT_STEPS = {1: {4: [("q",)]}, 2: {3: [("k",)]}, 4: {3: [("y", 0)]}, 5: {1: [("z", 0)], 3: [("a", 0)]},
             6: {3: [("y", 1)]}, 7: {0: [("z", 1)], 2: [("a", 1)], 4: [("q",)]}, 8: {3: [("k",)]},
             10: {3: [("y", 2)]}, 11: {1: [("z", 2)], 3: [("a", 2)]},
             12: {0: [("y", 3)], 1: [("z", 3)], 3: [("a", 3)]}}
DVE_STEPS = {3: {1: [("probs", 0)]}, 4: {3: [("norm", 0)]}, 5: {1: [("probs", 1)], 3: [("lo", 0)]},
             6: {3: [("norm", 1)]}, 7: {2: [("lo", 1)]},
             9: {1: [("probs", 2)]}, 10: {3: [("norm", 2)]}, 11: {1: [("probs", 3)], 3: [("lo", 2)]},
             12: {0: [("norm", 3)], 3: [("lo", 3)]}}


def program(nc, x_in, c_in, ada_w, ada_b, norm_g, pool_w, pool_scale, ret_w_in, ret_w_out, mlp_w1, mlp_w2,
            final_g, ident_in, cos_in, sin_in, decay_in, rcount_in, out):
    with ExitStack() as ctx:
        def sb(name, shape, dt=F32):
            return ctx.enter_context(nc.sbuf_tensor(name, shape, dt))

        def sem(name):
            return ctx.enter_context(nc.semaphore(name))

        raw = sb("raw", [P, RING, CK, NB])
        w_hi = sb("w_hi", [P, RING, CK, NB], F32R)
        w_lo = sb("w_lo", [P, RING, CK, NB], F32R)
        ada_raw = sb("ada_raw", [P, RING, AW])
        ada_acc = sb("ada_acc", [P, D])
        x = sb("x", [P, TT, D])
        h_hi = sb("h_hi", [P, KT, S], F32R)
        h_lo = sb("h_lo", [P, KT, S], F32R)
        a_hi = sb("a_hi", [P, KT, S], F32R)
        a_lo = sb("a_lo", [P, KT, S], F32R)
        gate = sb("gate", [P, D])
        ev = sb("ev", [P, 2, TT, NB])
        ident = sb("ident", [P, P])
        ones = sb("ones", [P, P])
        diag = sb("diag", [P, TT, P])
        rows = sb("rows", [P, 3, P])
        bias_col = sb("bias_col", [P, 8, KT])
        norm_col = sb("norm_col", [P, 4, KT])
        mod_col = sb("mod_col", [P, 8, KT])
        gain_col = sb("gain_col", [P, 4, KT])
        cond = sb("cond", [P, KT])
        rcount = sb("rcount", [P, 4, 16])
        sq_junk = sb("sq_junk", [P, TT, NB], mybir.dt.bfloat16)
        ssq = sb("ssq", [P, TT, 4])
        ssum = sb("ssum", [P, TT])
        meansq = sb("meansq", [P, TT])
        rstd = sb("rstd", [P, TT])
        minus_half = sb("minus_half", [P, TT])
        y_stats = sb("y_stats", [P, TT, 6])
        y_mv = sb("y_mv", [P, TT, 2])
        y_var = sb("y_var", [P, TT])
        y_rstd = sb("y_rstd", [P, TT])
        scratch = sb("scratch", [P, 8192 + 384])
        h32 = scratch[:, 0:4096].rearrange("p (k t) -> p k t", k=KT)
        win = [scratch[:, 4096 + 1024 * i:5120 + 1024 * i].rearrange("p (k t) -> p k t", k=4) for i in range(2)]
        layer_scale = scratch[:, 6144:8192]
        hbuf = [scratch[:, 512 * i:512 * (i + 1)].rearrange("p (k t) -> p k t", k=2) for i in range(2)]
        ybuf = scratch[:, 0:1024].rearrange("p (t n) -> p t n", t=TT)
        rot_a = scratch[:, 1024:1536]
        rot_b = scratch[:, 1536:2048]
        rot = scratch[:, 2048:3072].rearrange("p (t n) -> p t n", t=TT)
        qT = scratch[:, 3072:4096].rearrange("p (k t) -> p k t", k=4)
        kT = scratch[:, 4096:5120].rearrange("p (k t) -> p k t", k=4)
        decay = scratch[:, 5120:7168].rearrange("p (h t) -> p h t", h=HEADS)
        cos = scratch[:, 7168:7680].rearrange("p (t i) -> p t i", t=TT)
        sin = scratch[:, 7680:8192].rearrange("p (t i) -> p t i", t=TT)
        probs = scratch[:, 8192:8192 + 384]
        final_gain = scratch[:, 4096:6144]

        acc = [[ctx.enter_context(nc.psum_tensor(f"acc{p}{t}", [P, NB], F32)) for t in range(TT)] for p in range(2)]
        tb = [ctx.enter_context(nc.psum_tensor(f"tb{i}", [P, NB], F32)) for i in range(2)]
        mod_ps = ctx.enter_context(nc.psum_tensor("mod_ps", [P, NB], F32))
        score_ps = ctx.enter_context(nc.psum_tensor("score_ps", [P, NB], F32))

        raw_in = [sem(f"raw_in{i}") for i in range(RING)]
        ada_in = [sem(f"ada_in{i}") for i in range(RING)]
        x_loaded = sem("x_loaded")
        rows_in = sem("rows_loaded")
        const_in = sem("const_loaded")
        bias_in = sem("gate_bias_loaded")
        ret_in = sem("ret_tables_loaded")
        scale_in = sem("layer_scale_loaded")
        final_in = sem("final_g_loaded")
        out_done = sem("out_done")
        rows_zero = sem("rows_zero")
        ones_set = sem("ones_set")
        half_set = sem("half_set")
        cond_rows = sem("cond_rows")
        setup_T = sem("setup_transposed")
        setup_col = sem("setup_columns")
        hi_ready = sem("hi_ready")
        lo_ready = sem("lo_ready")
        w_used = sem("w_used")
        evac = sem("evac_done")
        sq_done = sem("squared")
        tr_done = sem("tr_bank_filled")
        tevac = sem("tr_bank_evacuated")
        tlo = sem("tr_bank_split")
        mul_done = sem("gated")
        x_added = sem("x_added")
        ab_done = sem("rot_products")
        rot_done = sem("rotated")
        score_done = sem("scores")
        prob_done = sem("probs")
        y_ready = sem("y_summed")
        bn_done = sem("y_stats_done")
        mv_done = sem("y_mv_done")
        var_done = sem("y_var_done")
        z_rstd = sem("y_rstd_done")
        z_mul = sem("z_gated")
        z_done = sem("z_scaled")
        ada_done = sem("ada_done")
        acc_clear = sem("ada_acc_clear")
        col_mm = sem("col_summed")
        col_used = sem("mod_col_ready")
        gate_mm = sem("gate_summed")
        gate_ready = sem("gate_ready")
        gate_part = sem("gate_part")
        gain_ready = sem("gain_ready")
        ssq_done = sem("ssq_done")
        ssum_done = sem("ssum_done")
        ms_done = sem("meansq_done")
        rstd_done = sem("rstd_done")
        diag_ready = sem("diag_ready")
        hhi_done = sem("h_hi_done")
        h_ready = sem("h_ready")
        pool_step = sem("pool_step")
        p_ready = sem("p_ready")
        p_hi = sem("p_hi")
        p_lo = sem("p_lo")
        xn_done = sem("x_normed")
        o_ready = sem("out_ready")

        block = ctx.enter_context(nc.Block())

        def rows_of(weights, chunk, col):
            return weights[chunk * CK * P:(chunk + 1) * CK * P, col].rearrange("(k p) n -> p k n", p=P)

        @block.sync
        def _(sp):
            n = Count()
            ada_flat = ada_w.rearrange("i s d (j k) -> (i s) d j k", j=3)

            def load_chunk(c, source):
                if n.reg is not None or CH * n.of("U") + c >= RING:
                    sp.wait_ge(lo_ready, n.of("U") * CH + (c - RING + 1))
                sp.dma_start(raw[:, c % RING], source).then_inc(raw_in[c % RING], 16)

            def load_ada(seg, a):
                if n.reg is not None or n.of("AD") >= RING:
                    sp.wait_ge(ada_done, n.of("AD") - (RING - 1))
                norm, part = (seg // 3, seg % 3) if isinstance(seg, int) else seg
                src = ada_flat[norm, (a // 2) * P:(a // 2 + 1) * P, bass.ds(part, 1),
                               (a % 2) * AW:(a % 2 + 1) * AW].rearrange("p j k -> p (j k)")
                sp.dma_start(ada_raw[:, a % RING], src).then_inc(ada_in[a % RING], 16)
                n.add(AD=1)

            def unit(kind, source, seg, a0, count):
                behind = {c: [] for c in range(CH)}
                for j in range(count):
                    step = next(s for s in range(CH) if count * (s + 1) // CH > j)
                    behind[min(CH - 1, step + 2)].append(a0 + j)
                for c in range(CH):
                    load_chunk(c, source(c))
                    for a in behind[c]:
                        load_ada(seg, a)
                n.unit(kind)

            def rows_of(weights, col):
                return lambda c: weights[c * CK * P:(c + 1) * CK * P, col].rearrange("(k p) n -> p k n", p=P)

            def group_rows_of(weights, g, block_):
                grouped = weights.rearrange("(g k p) n -> g p k n", k=KT, p=P)
                return lambda c: grouped[bass.ds(g, 1), :, c * CK:(c + 1) * CK,
                                         block_ * NB:(block_ + 1) * NB].rearrange("g p k n -> p (g k) n")

            sp.wait_ge(rows_zero, 1)
            sp.dma_start(rows[0:KT, 2, :], c_in.rearrange("b (k p) -> (b k) p", p=P)).then_inc(rows_in, 16)
            sp.dma_start(rows[0:64, 1, :], norm_g.rearrange("i s (k p) -> (i s k) p", p=P)).then_inc(rows_in, 16)
            bias_rows = ada_b.rearrange("i s (j p) -> (i s) j p", p=P)
            for i in range(4):
                sp.dma_start(rows[2 * KT * i:2 * KT * (i + 1), 0, :], bias_rows[i, 0:2 * KT, :]).then_inc(rows_in, 16)
            sp.dma_start(ident[:], ident_in).then_inc(const_in, 16)
            sp.dma_start(rcount[:], rcount_in).then_inc(const_in, 16)
            for a in range(RING):
                load_ada(0, a)
            for t in range(TT):
                sp.dma_start(x[:, t, :], x_in[0, t * P:(t + 1) * P, :]).then_inc(x_loaded, 16)
            for a in range(RING, SEG):
                load_ada(0, a)
            for a in range(SEG):
                load_ada(1, a)
            pool_rows = rows_of(pool_w.rearrange("l g c n -> (l g c) n"), slice(0, NB))
            for c in range(RING):
                load_chunk(c, pool_rows(c))
            for a in range(SEG):
                load_ada(2, a)
            for a in range(SEG):
                load_ada(3, a)
                if a % 4 == 3 and a < 16:
                    load_chunk(RING + a // 4, pool_rows(RING + a // 4))
            for a in range(SEG):
                load_ada(4, a)
            n.add(U=1)

            def mlp(layer):
                for first, trips, plan in MLP_PLAN[layer]:
                    spread, what = plan
                    kept_seg = {(0, 0): 5, (0, 3): 8, (1, 0): 11}.get((layer, first))

                    def group(g, seg):
                        for u in range(M_UNITS):
                            if u < 4:
                                source = rows_of(mlp_w1[layer], bass.ds(g * (4 * NB) + u * NB, NB))
                            else:
                                source = group_rows_of(mlp_w2[layer], g, u - 4)
                            unit(M_KINDS[u], source, seg, sum(spread[:u]), spread[u])

                    if trips == 1:
                        group(first, kept_seg)
                    else:
                        with sp.Fori(0, trips) as r:
                            n.enter(r, mlp_round(plan))
                            group(r + first, (2, r))
                        n.leave(trips)

            def retention():
                with sp.Fori(0, 2) as r:
                    n.enter(r, R_ROUND)
                    for i, kind in enumerate(R_KINDS):
                        pair, w = i // 6, i % 6
                        if kind == "m2":
                            source = group_rows_of(ret_w_out[0], r, i - 12)
                        else:
                            if kind in "qk":
                                col = r * (2 * NB) + (D * (kind == "k") + pair * NB)
                            else:
                                col = r * (GROUP_HEADS * NB) + (2 * D + 2 * D * (kind == "g") +
                                                                (2 * pair + (w - 2) // 2) * NB)
                            source = rows_of(ret_w_in[0], bass.ds(col, NB))
                        unit(kind, source, (3, r), 2 * i, 2)
                n.leave(2)

            mlp(0)
            retention()
            mlp(1)
            for t in range(TT):
                sp.wait_ge(o_ready, t + 1)
                sp.dma_start(out[0, t * P:(t + 1) * P, :], x[:, t, :]).then_inc(out_done, 16)
            sp.wait_ge(out_done, 16 * TT)

        @block.tensor
        def _(pe):
            n = Count()

            def chunk(c, lhs_hi, lhs_lo, pair, first, last):
                for j in range(CK):
                    for t in range(TT):
                        tok = slice(t * P, (t + 1) * P)
                        for i, (l, w) in enumerate(((lhs_lo, w_hi), (lhs_hi, w_lo), (lhs_hi, w_hi))):
                            mm = nc.tensor.matmul(acc[pair][t][:], l[:, CK * c + j, tok], w[:, c % RING, j, :],
                                                  start=first and j == 0 and i == 0,
                                                  stop=last and j == CK - 1 and i == 2)
                mm.then_inc(w_used, 1)

            def unit(kind, pair, hooks, lhs, ready):
                for c in range(CH):
                    pe.wait_ge(lo_ready, n.of("U") * CH + (c + 1))
                    ready(c)
                    if c == 0:
                        pe.wait_ge(evac, (n.of("E") - 1) * TT)
                    chunk(c, *lhs, pair, c == 0, c == CH - 1)
                    for hook in hooks.get(c, []):
                        hook()
                n.unit(kind)

            def transposes(source, split):
                for b in range(2):
                    pe.wait_ge(tevac, n.of("TB") + (b - 1))
                    pe.wait_ge(tlo, n.of("TL"))
                    for j in range(2):
                        for t in range(TT):
                            m = 2 * b + j
                            tr = nc.tensor.transpose(tb[b][:, j * S + t * P:j * S + (t + 1) * P],
                                                     source(t)[:, m * P:(m + 1) * P], ident[:])
                    tr.then_inc(tr_done, 1)
                n.add(TB=2, TL=2 if split else 0)

            def mod_bank_free():
                if n.n["CS"]:
                    pe.wait_ge(col_used, n.of("CS"))
                if n.n["GB"]:
                    pe.wait_ge(gate_ready, n.of("GB"))

            def column_sums():
                pe.wait_ge(ada_done, n.of("AD"))
                mod_bank_free()
                for k in range(KT):
                    mm = nc.tensor.matmul(mod_ps[:, k:k + 1], ada_acc[:, k * P:(k + 1) * P], ones[:, 0:1],
                                          start=True, stop=True)
                mm.then_inc(col_mm, 1)
                n.add(CS=1)

            def gate_sum(b):
                pe.wait_ge(ada_done, n.of("AD"))
                mod_bank_free()
                nc.tensor.matmul(mod_ps[:], ones[:], ada_acc[:, b * NB:(b + 1) * NB], start=True,
                                 stop=True).then_inc(gate_mm, 1)
                n.add(GB=1)

            def norm():
                pe.wait_ge(diag_ready, n.of("NO") + 1)
                for f in range(KT // 2):
                    if n.of("TB") >= 2:
                        pe.wait_ge(tevac, n.of("TB") - 1)
                    if f < 2 and n.of("TL"):
                        pe.wait_ge(tlo, n.of("TL"))
                    for j in range(2):
                        for t in range(TT):
                            k = 2 * f + j
                            tr = nc.tensor.matmul(tb[f % 2][:, j * S + t * P:j * S + (t + 1) * P],
                                                  x[:, t, k * P:(k + 1) * P], diag[:, t, :], start=True, stop=True)
                    tr.then_inc(tr_done, 1)
                    n.add(TB=1)
                n.add(NO=1)

            pe.wait_ge(const_in, 32)
            pe.wait_ge(cond_rows, 1)
            for i in range(3):
                tr = nc.tensor.transpose(tb[0][:, i * P:(i + 1) * P], rows[:, i, :], ident[:])
            tr.then_inc(setup_T, 1)
            pe.wait_ge(ones_set, 1)
            pe.wait_ge(setup_col, 1)
            for seg in range(2):
                n.add(AD=SEG)
                column_sums()
            norm()
            n.add(AD=SEG)
            for b in range(4):
                gate_sum(b)
            for gi in range(4):
                for c in (2 * gi, 2 * gi + 1):
                    pe.wait_ge(lo_ready, c + 1)
                    if c == 2 * gi:
                        pe.wait_ge(p_lo, gi + 1)
                        if gi >= 2:
                            pe.wait_ge(evac, (gi - 1) * TT)
                    chunk(c, a_hi, a_lo, gi % 2, c == 2 * gi, c == 2 * gi + 1)
            n.add(U=1, E=4)
            n.add(AD=SEG)
            column_sums()
            n.add(AD=SEG)
            column_sums()

            def ready_h(c):
                pe.wait_ge(h_ready, n.n["HT"] - CH + c + 1)

            def mlp(layer):
                norm()
                n.add(HT=CH)
                for first, trips, plan in MLP_PLAN[layer]:
                    spread, what = plan

                    def group():
                        split0 = n.of("TL")
                        for u in range(M_UNITS):
                            hooks = {}
                            if 1 <= u <= 4:
                                def transpose_squares(pair=(u - 1) % 2):
                                    pe.wait_ge(sq_done, n.of("SQ") * TT)
                                    transposes(lambda t: ev[:, pair, t, :], True)
                                hooks[2] = [transpose_squares]
                            if u < 4:
                                unit("m1", u % 2, hooks, (h_hi, h_lo), ready_h)
                            else:
                                unit("m2", u % 2, hooks, (a_hi, a_lo), lambda c: pe.wait_ge(tlo, split0 + (c + 1)))
                            n.add(AD=spread[u])
                            if what == "now" and u >= 4:
                                gate_sum(u - 4)
                        if what == "col":
                            column_sums()

                    if trips == 1:
                        group()
                    else:
                        with pe.Fori(0, trips) as r:
                            n.enter(r, mlp_round(plan))
                            group()
                        n.leave(trips)

            def scores(hd):
                pe.wait_ge(tevac, n.of("TB"))
                if hd:
                    pe.wait_ge(prob_done, n.of("SC"))
                w = (hd % 2) * 2
                for part, q0 in ((0, 0), (1, P)):
                    for j in range(2):
                        mm = nc.tensor.matmul(score_ps[:, part * S:part * S + S - q0],
                                              kT[:, w + j, part * P:(part + 1) * P], qT[:, w + j, q0:S],
                                              start=j == 0, stop=j == 1)
                mm.then_inc(score_done, 1)
                n.add(SC=1)

            def weigh(pair):
                pe.wait_ge(prob_done, n.of("Y") + 1)
                pe.wait_ge(evac, n.of("E") * TT)
                nc.tensor.matmul(acc[pair][0][:], probs[:, 0:P], ev[:, 1, 0, :], start=True, stop=True)
                nc.tensor.matmul(acc[pair][1][:], probs[:, P:S], ev[:, 1, 0, :], start=True, stop=False)
                nc.tensor.matmul(acc[pair][1][:], probs[:, S:S + P], ev[:, 1, 1, :], start=False,
                                 stop=True).then_inc(y_ready, 1)
                n.add(E=1, Y=1)

            def transpose_rotated():
                pe.wait_ge(rot_done, n.of("RO") * TT)
                transposes(lambda t: rot[:, t, :], False)

            def transpose_z():
                pe.wait_ge(z_done, n.of("Y"))
                transposes(lambda t: ybuf[:, t, :], True)

            def retention():
                norm()
                for b in range(4):
                    gate_sum(b)
                n.add(HT=CH)
                with pe.Fori(0, 2) as r:
                    n.enter(r, R_ROUND)
                    split0 = n.of("TL")
                    for i, kind in enumerate(R_KINDS):
                        hooks = {}
                        for c, steps in PE_STEPS.get(i, {}).items():
                            hooks[c] = [transpose_rotated if s == "T rot" else transpose_z if s == "T z" else
                                        (lambda s=s, i=i: scores(s[1]) if s[0] == "scores" else weigh((i - 1) % 2))
                                        for s in steps]
                        if kind == "m2":
                            unit(kind, i % 2, hooks, (a_hi, a_lo), lambda c: pe.wait_ge(tlo, split0 + (c + 1)))
                        else:
                            unit(kind, i % 2, hooks, (h_hi, h_lo), ready_h)
                        n.add(AD=2)
                    column_sums()
                n.leave(2)

            mlp(0)
            retention()
            mlp(1)

        @block.scalar
        def _(act):
            n = Count()

            def hi(c, ahead=0):
                u = n.of("U") + ahead
                if c % 1 == 0:
                    act.wait_ge(raw_in[c % RING], (u * 2 + (c // RING + 1)) * 16)
                if not (n.reg is None and u * CH + c < RING):
                    act.wait_ge(w_used, u * CH + (c - RING + 1))
                nc.scalar.activation(w_hi[:, c % RING], raw[:, c % RING], ACT.Copy).then_inc(hi_ready, 1)

            def steps(hooks):
                for s in range(CH):
                    if s < CH - LEAD:
                        hi(s + LEAD)
                    elif not (ending[0]):
                        hi(s + LEAD - CH, 1)
                    for hook in hooks.get(s, []):
                        hook()

            ending = [False]

            def evacuate(pair, func, target, counts=True):
                for t in range(TT):
                    nc.scalar.activation(target[:, t, :], acc[pair][t][:], func).then_inc(evac, 1)
                n.add(E=1)

            def evacuate_T(targets, b):
                act.wait_ge(tr_done, n.of("TB") + 1)
                nc.scalar.activation(targets, tb[b][:].rearrange("p (k t) -> p k t", k=2), ACT.Copy).then_inc(tevac, 1)
                n.add(TB=1)

            def squares(block_):
                for t in range(TT):
                    if n.reg is not None or n.of("SB"):
                        act.wait_ge(ssq_done, (n.of("SB") - 1) * TT + t + 1)
                    nc.scalar.activation(sq_junk[:, t, :], x[:, t, block_ * NB:(block_ + 1) * NB], ACT.Square,
                                         accum_out=ssq[:, t, block_:block_ + 1]).then_inc(ssq_done, 1)
                n.add(SB=1)

            def unit_done():
                act.wait_ge(w_used, (n.of("U") + 1) * CH)

            def norm(target_of):
                k0 = n.n["NO"]
                act.wait_ge(gain_ready, k0 + 1)
                for f in range(KT // 2):
                    act.wait_ge(tr_done, n.of("TB") + 1)
                    target = target_of(f)
                    for j in range(2):
                        k = 2 * f + j
                        h = nc.scalar.activation(target[:, j, :], tb[f % 2][:, j * S:(j + 1) * S], ACT.Identity,
                                                 bias=mod_col[:, 2 * k0, k:k + 1], scale=gain_col[:, k0, k:k + 1])
                    h.then_inc(tevac, 1)
                    n.add(TB=1)
                n.add(NO=1)

            def norm_by_banks():
                h0 = n.n["HT"]

                def target_of(f):
                    if f >= 2:
                        act.wait_ge(h_ready, h0 + f - 1)
                    return hbuf[f % 2]
                norm(target_of)
                n.add(HT=CH)

            def load_gate_bias(seg):
                row = ada_b.rearrange("i s k -> (i s) k")[seg:seg + 1, 2 * D:3 * D]
                act.dma_start(gate[:], row.to_broadcast([P, D])).then_inc(bias_in, 16)

            load_gate_bias(0)
            act.dma_start(layer_scale, pool_scale.to_broadcast([P, D])).then_inc(scale_in, 16)
            act.wait_ge(rows_in, 16 * 6)
            nc.scalar.activation(rows[:, 2, :], rows[:, 2, :], ACT.Silu).then_inc(cond_rows, 1)
            act.wait_ge(x_loaded, 16 * TT)
            for b in range(4):
                squares(b)
            norm(lambda f: h32[:, 2 * f:2 * f + 2, :])
            for c in range(LEAD):
                hi(c)
            for gi in range(4):
                act.wait_ge(p_ready, gi + 1)
                nc.scalar.activation(a_hi[:, 4 * gi:4 * gi + 4, :], win[(gi + 1) % 2], ACT.Copy).then_inc(p_hi, 1)
            for c in range(LEAD, CH):
                hi(c)
            for gi in range(4):
                act.wait_ge(w_used, 2 * gi + 2)
                if gi >= 2:
                    act.wait_ge(x_added, (gi - 1) * TT)
                evacuate(gi % 2, ACT.Copy, ev[:, gi % 2])
            act.wait_ge(x_added, 4 * TT)
            n.add(XA=4)
            load_gate_bias(1)
            for b in range(4):
                squares(b)
            for c in range(LEAD):
                hi(c, 1)
            n.add(U=1)

            def mlp(layer):
                norm_by_banks()
                for first, trips, plan in MLP_PLAN[layer]:
                    def group(end):
                        for u in range(M_UNITS):
                            hooks = {}
                            if 1 <= u <= 4:
                                def upper(u=u):
                                    for b in range(2):
                                        k = 4 * (u - 1) + 2 * b
                                        evacuate_T(a_hi[:, k:k + 2, :], b)
                                hooks[2] = [upper]
                            if u > 4:
                                def block_squares(u=u):
                                    act.wait_ge(x_added, n.of("XA") * TT)
                                    squares(u - 5)
                                hooks[2] = [block_squares]
                            ending[0] = end and u == M_UNITS - 1
                            steps(hooks)
                            unit_done()
                            if u < 4:
                                if u < 2:
                                    act.wait_ge(x_added, (n.of("XA") - (1 - u)) * TT)
                                evacuate(u % 2, ACT.Relu, ev[:, u % 2])
                                for t in range(TT):
                                    act.wait_ge(evac, (n.of("E") - 1) * TT + t + 1)
                                    nc.scalar.activation(ev[:, u % 2, t, :], ev[:, u % 2, t, :],
                                                         ACT.Square).then_inc(sq_done, 1)
                            else:
                                if u >= 6:
                                    act.wait_ge(x_added, (n.of("XA") - 1) * TT)
                                evacuate(u % 2, ACT.Copy, ev[:, u % 2])
                            n.unit(M_KINDS[u])
                            n.add(E=-1)

                    if trips == 1:
                        group(layer == 1 and first == 3)
                    else:
                        with act.Fori(0, trips) as r:
                            n.enter(r, mlp_round(plan))
                            group(False)
                        n.leave(trips)

            def between():
                act.wait_ge(x_added, n.of("XA") * TT)
                squares(3)

            def retention():
                act.dma_start(decay, decay_in).then_inc(ret_in, 16)
                act.dma_start(cos, cos_in).then_inc(ret_in, 16)
                act.dma_start(sin, sin_in).then_inc(ret_in, 16)
                norm_by_banks()
                with act.Fori(0, 2) as r:
                    n.enter(r, R_ROUND)
                    for i, kind in enumerate(R_KINDS):
                        hooks = {s: [lambda what=w, i=i: step(what, i) for w in ws]
                                 for s, ws in ACT_STEPS.get(i, {}).items()}
                        if i > 12:
                            def block_squares(i=i):
                                act.wait_ge(x_added, n.of("XA") * TT)
                                squares(i - 13)
                            hooks[2] = [block_squares]
                        steps(hooks)
                        unit_done()
                        if i < 2:
                            act.wait_ge(x_added, (n.of("XA") - (1 - i)) * TT)
                        elif i in (2, 8):
                            act.wait_ge(rot_done, (n.of("RO") - 1) * TT)
                        elif i in (3, 9):
                            act.wait_ge(rot_done, n.of("RO") * TT)
                        elif i in (4, 6, 10, 12):
                            act.wait_ge(z_mul, n.of("Y") * TT)
                        elif i >= 14:
                            act.wait_ge(x_added, (n.of("XA") - 1) * TT)
                        evacuate(i % 2, ACT.Silu if kind == "g" else ACT.Copy, ev[:, i % 2])
                        n.unit(kind)
                        n.add(E=-1)
                n.leave(2)

            def step(what, i):
                if what[0] in ("q", "k"):
                    target = qT if what[0] == "q" else kT
                    for b in range(2):
                        evacuate_T(target[:, 2 * b:2 * b + 2, :], b)
                elif what[0] == "a":
                    for b in range(2):
                        k = 4 * what[1] + 2 * b
                        evacuate_T(a_hi[:, k:k + 2, :], b)
                elif what[0] == "y":
                    act.wait_ge(y_ready, n.of("Y") + 1)
                    evacuate((i - 1) % 2, ACT.Copy, ybuf)
                    n.add(Y=1)
                else:
                    act.wait_ge(z_mul, n.of("Y") * TT)
                    act.wait_ge(z_rstd, n.of("Y"))
                    for t in range(TT):
                        z = nc.scalar.activation(ybuf[:, t, :], ybuf[:, t, :], ACT.Copy, scale=y_rstd[:, t:t + 1])
                    z.then_inc(z_done, 1)

            mlp(0)
            between()
            load_gate_bias(2)
            retention()
            between()
            load_gate_bias(3)
            act.dma_start(final_gain, final_g.rearrange("(a n) -> a n", a=1).to_broadcast([P, D])).then_inc(final_in, 16)
            mlp(1)
            between()
            act.wait_ge(rstd_done, 5)
            for t in range(TT):
                nc.scalar.activation(x[:, t, :], x[:, t, :], ACT.Copy, scale=rstd[:, t:t + 1]).then_inc(xn_done, 1)

        @block.vector
        def _(dve):
            n = Count()

            def lo(c, ahead=0):
                dve.wait_ge(hi_ready, (n.of("U") + ahead) * CH + (c + 1))
                nc.vector.tensor_tensor(w_lo[:, c % RING], raw[:, c % RING], w_hi[:, c % RING].bitcast(F32),
                                        ALU.subtract).then_inc(lo_ready, 1)

            def ada(a):
                if a < 2:
                    dve.wait_ge(acc_clear, n.of("SG") + 1)
                else:
                    dve.wait_ge(ada_done, n.of("AD") - 1)
                dve.wait_ge(ada_in[a % RING], (ada_round() + (a // RING + 1)) * 16)
                part = ada_acc[:, (a % 2) * AW:(a % 2 + 1) * AW]
                nc.vector.scalar_tensor_tensor(out=part, in0=ada_raw[:, a % RING], scalar=cond[:, a // 2:a // 2 + 1],
                                               in1=part, op0=ALU.mult, op1=ALU.add).then_inc(ada_done, 1)
                n.add(AD=1)
                if a == SEG - 1:
                    n.add(SG=1)

            def ada_round():
                return n.of("SG") * (SEG // RING)

            def steps(hooks, a0, count, end=False):
                done = 0
                for s in range(CH):
                    if s < CH - LEAD:
                        lo(s + LEAD)
                    elif not end:
                        lo(s + LEAD - CH, 1)
                    while done < count * (s + 1) // CH:
                        ada(a0 + done)
                        done += 1
                    for hook in hooks.get(s, []):
                        hook()

            def columns(index):
                dve.wait_ge(col_mm, n.of("CS") + 1)
                nc.vector.tensor_tensor(mod_col[:, index, :].rearrange("p s k -> p (s k)"), mod_ps[:, 0:KT],
                                        bias_col[:, index, :].rearrange("p s k -> p (s k)"),
                                        ALU.add).then_inc(col_used, 1)
                n.add(CS=1)

            def gate_block(b):
                blk = gate[:, b * NB:(b + 1) * NB]
                dve.wait_ge(gate_mm, n.of("GB") + 1)
                dve.wait_ge(bias_in, 16 * (n.of("GB") // 4 + 1))
                nc.vector.tensor_tensor(blk, mod_ps[:], blk, ALU.add).then_inc(gate_ready, 1)
                n.add(GB=1)

            def add_block(p, b):
                blk = slice(b * NB, (b + 1) * NB)
                for t in range(TT):
                    dve.wait_ge(evac, n.of("E") * TT + (t + 1))
                    nc.vector.tensor_tensor(ev[:, p, t, :], ev[:, p, t, :], gate[:, blk],
                                            ALU.mult).then_inc(mul_done, 1)
                for t in range(TT):
                    dve.wait_ge(mul_done, n.of("XA") * TT + (t + 1))
                    nc.vector.tensor_tensor(x[:, t, blk], x[:, t, blk], ev[:, p, t, :], ALU.add).then_inc(x_added, 1)

            def lower_T(k, b):
                dve.wait_ge(tevac, n.of("TB") + 1)
                nc.vector.tensor_tensor(a_lo[:, k:k + 2, :], tb[b][:].rearrange("p (k t) -> p k t", k=2),
                                        a_hi[:, k:k + 2, :].bitcast(F32), ALU.subtract).then_inc(tlo, 1)
                n.add(TB=1)

            def mean_square():
                m = n.n["NO"]
                n.add(SB=4 if m < 2 else 1)
                dve.wait_ge(ssq_done, n.n["SB"] * TT)
                nc.vector.tensor_reduce(ssum[:], ssq[:], AX_X, ALU.add).then_inc(ssum_done, 1)
                dve.wait_ge(ssum_done, m + 1)
                nc.vector.tensor_scalar(meansq[:], ssum[:], 1.0 / D, EPS, ALU.mult, ALU.add).then_inc(ms_done, 1)

            def diagonals():
                m = n.n["NO"]
                dve.wait_ge(rstd_done, m + 1)
                for t in range(TT):
                    d = nc.vector.tensor_scalar(diag[:, t, :], ident[:], rstd[:, t:t + 1], None, ALU.mult)
                d.then_inc(diag_ready, 1)

            def gains():
                m = n.n["NO"]
                dve.wait_ge(col_used, 2 * (m + 1))
                nc.vector.scalar_tensor_tensor(out=gain_col[:, m, :], in0=mod_col[:, 2 * m + 1, :], scalar=1.0,
                                               in1=norm_col[:, m, :], op0=ALU.add,
                                               op1=ALU.mult).then_inc(gain_ready, 1)
                n.add(NO=1)

            def split_h():
                h0 = n.n["HT"]

                def lower(f):
                    dve.wait_ge(hhi_done, h0 + f + 1)
                    nc.vector.tensor_tensor(h_lo[:, 2 * f:2 * f + 2, :], hbuf[f % 2],
                                            h_hi[:, 2 * f:2 * f + 2, :].bitcast(F32),
                                            ALU.subtract).then_inc(h_ready, 1)
                for f in range(KT // 2):
                    dve.wait_ge(tevac, n.of("TB") + 1)
                    n.add(TB=1)
                    nc.vector.tensor_copy(h_hi[:, 2 * f:2 * f + 2, :], hbuf[f % 2]).then_inc(hhi_done, 1)
                    if f:
                        lower(f - 1)
                lower(KT // 2 - 1)
                n.add(HT=CH)

            dve.wait_ge(setup_T, 1)
            nc.vector.tensor_copy(bias_col[:].rearrange("p s k -> p (s k)"), tb[0][:, 0:P])
            nc.vector.tensor_copy(norm_col[:].rearrange("p s k -> p (s k)"), tb[0][:, P:P + 4 * KT])
            nc.vector.tensor_copy(cond[:], tb[0][:, 2 * P:2 * P + KT]).then_inc(setup_col, 1)
            dve.wait_ge(setup_col, 1)
            for a in range(8):
                ada(a)
            mean_square()
            for a in range(8, 16):
                ada(a)
            diagonals()
            for a in range(16, SEG):
                ada(a)
            columns(slice(0, 1))
            for a in range(SEG):
                ada(a)
            columns(slice(1, 2))
            gains()
            for c in range(LEAD):
                lo(c)
            n.add(TB=CH)

            pool_count = [0]
            gate_chunks = iter(range(SEG))

            def pool_op(ins, behind=1):
                ins.then_inc(pool_step, 1)
                pool_count[0] += 1
                for _ in range(behind):
                    a = next(gate_chunks, None)
                    if a is not None:
                        ada(a)

            def own():
                dve.wait_ge(pool_step, pool_count[0])

            dve.wait_ge(tevac, CH)
            for gi, w in enumerate(WINDOWS):
                h = h32[:, 4 * gi:4 * gi + 4, :]
                cur, at, s = h, 0, 1
                at = 0
                while s < w:
                    dst = win[at]
                    if s > 1:
                        own()
                    pool_op(nc.vector.tensor_tensor(dst[:, :, s:], cur[:, :, s:], cur[:, :, :S - s], ALU.add), 1)
                    pool_op(nc.vector.tensor_copy(dst[:, :, :s], cur[:, :, :s]), 0)
                    cur, at, s = dst, 1 - at, 2 * s
                p = win[at]
                assert at == (gi + 1) % 2
                own()
                pool_op(nc.vector.scalar_tensor_tensor(out=p, in0=cur, scalar=1.0 / w, in1=h, op0=ALU.mult,
                                                       op1=ALU.subtract))
                own()
                pool_op(nc.vector.tensor_tensor(p[:, :, :w], cur[:, :, :w], rcount[:, :, :w], ALU.mult), 1)
                own()
                nc.vector.tensor_tensor(p[:, :, :w], p[:, :, :w], h[:, :, :w], ALU.subtract).then_inc(p_ready, 1)
                ada_next = next(gate_chunks, None)
                if ada_next is not None:
                    ada(ada_next)
                dve.wait_ge(p_hi, gi + 1)
                nc.vector.tensor_tensor(a_lo[:, 4 * gi:4 * gi + 4, :], p,
                                        a_hi[:, 4 * gi:4 * gi + 4, :].bitcast(F32), ALU.subtract).then_inc(p_lo, 1)
                dve.wait_ge(p_lo, gi + 1)
            for a in gate_chunks:
                ada(a)
            dve.wait_ge(scale_in, 16)
            for b in range(4):
                gate_block(b)
                dve.wait_ge(gate_ready, b + 1)
                blk = slice(b * NB, (b + 1) * NB)
                nc.vector.tensor_tensor(gate[:, blk], gate[:, blk], layer_scale[:, blk], ALU.mult).then_inc(gate_part, 1)
            dve.wait_ge(gate_part, 4)
            for c in range(LEAD, CH):
                for a in range(4 * (c - LEAD), 4 * (c - LEAD) + 4):
                    ada(a)
                lo(c)
            for gi in range(4):
                add_block(gi % 2, gi)
                n.add(E=1, XA=1)
                for a in range(16 + 4 * gi, 20 + 4 * gi):
                    ada(a)
            columns(slice(2, 3))
            mean_square()
            for a in range(8):
                ada(a)
            diagonals()
            for a in range(8, SEG):
                ada(a)
            for c in range(LEAD):
                lo(c, 1)
            columns(slice(3, 4))
            n.add(U=1)

            def mlp(layer):
                gains()
                split_h()
                for first, trips, plan in MLP_PLAN[layer]:
                    spread, what = plan

                    def group(r, end):
                        for u in range(M_UNITS):
                            hooks = {}
                            if 1 <= u <= 4:
                                def lower(u=u):
                                    for b in range(2):
                                        lower_T(4 * (u - 1) + 2 * b, b)
                                hooks[2] = [lower]
                            steps(hooks, sum(spread[:u]), spread[u], end and u == M_UNITS - 1)
                            if u >= 4:
                                if what == "now":
                                    gate_block(u - 4)
                                    dve.wait_ge(gate_ready, n.of("GB"))
                                add_block(u % 2, u - 4)
                            n.unit(M_KINDS[u])
                        n.add(SB=3)
                        if what == "col":
                            columns(bass.ds(r + 4, 1))

                    if trips == 1:
                        group(0, layer == 1 and first == 3)
                    else:
                        with dve.Fori(0, trips) as r:
                            n.enter(r, mlp_round(plan))
                            group(r, False)
                        n.leave(trips)

            def rotate(p, i):
                for t in range(TT):
                    src = ev[:, p, t, :].rearrange("p (h i) -> p h i", h=2)
                    dve.wait_ge(evac, n.of("E") * TT + (t + 1))
                    a3 = rot_a.rearrange("p (h i) -> p h i", h=2)
                    b3 = rot_b.rearrange("p (h i) -> p h i", h=2)
                    if t:
                        dve.wait_ge(rot_done, n.of("RO") * TT + t)
                    nc.vector.tensor_tensor(a3, src, cos[:, t:t + 1, :].to_broadcast([P, 2, 2 * P]), ALU.mult)
                    nc.vector.tensor_tensor(b3, src, sin[:, t:t + 1, :].to_broadcast([P, 2, 2 * P]),
                                            ALU.mult).then_inc(ab_done, 1)
                    dve.wait_ge(ab_done, n.of("RO") * TT + (t + 1))
                    a4 = rot_a.rearrange("p (h i two) -> p h i two", h=2, two=2)
                    b4 = rot_b.rearrange("p (h i two) -> p h i two", h=2, two=2)
                    o4 = rot[:, t, :].rearrange("p (h two i) -> p h two i", h=2, two=2)
                    nc.vector.tensor_tensor(o4[:, :, 0, :], a4[:, :, :, 0], b4[:, :, :, 1], ALU.subtract)
                    nc.vector.tensor_tensor(o4[:, :, 1, :], b4[:, :, :, 0], a4[:, :, :, 1],
                                            ALU.add).then_inc(rot_done, 1)

            def step(what, r):
                name, hd = what
                if name == "probs":
                    dve.wait_ge(score_done, n.of("SC") + 1)
                    table = decay[:, bass.ds(r * GROUP_HEADS + hd, 1), :].rearrange("p h t -> p (h t)")
                    nc.vector.tensor_tensor(probs[:, 0:S], score_ps[:, 0:S], table, ALU.mult)
                    nc.vector.tensor_tensor(probs[:, S:S + P], score_ps[:, S:S + P], table[:, 0:P],
                                            ALU.mult).then_inc(prob_done, 1)
                    n.add(SC=1)
                elif name == "norm":
                    for t in range(TT):
                        dve.wait_ge(evac, n.of("E") * TT + (t + 1))
                        nc.vector.bn_stats(y_stats[:, t, :], ybuf[:, t, :]).then_inc(bn_done, 1)
                    for t in range(TT):
                        dve.wait_ge(ret_in, 48)
                        dve.wait_ge(bn_done, n.of("Y") * TT + (t + 1))
                        nc.vector.bn_aggr(y_mv[:, t, :], y_stats[:, t, :]).then_inc(mv_done, 1)
                    dve.wait_ge(mv_done, (n.of("Y") + 1) * TT)
                    nc.vector.tensor_scalar(y_var[:], y_mv[:, :, 1], EPS, None, ALU.add).then_inc(var_done, 1)
                    for t in range(TT):
                        nc.vector.scalar_tensor_tensor(out=ybuf[:, t, :], in0=ybuf[:, t, :], scalar=y_mv[:, t, 0:1],
                                                       in1=ev[:, 0, t, :], op0=ALU.subtract,
                                                       op1=ALU.mult).then_inc(z_mul, 1)
                    n.add(E=1, Y=1)
                else:
                    for b in range(2):
                        lower_T(4 * hd + 2 * b, b)

            def retention():
                gains()
                split_h()
                for b in range(4):
                    gate_block(b)
                dve.wait_ge(gate_ready, n.of("GB"))
                dve.wait_ge(ret_in, 48)
                with dve.Fori(0, 2) as r:
                    n.enter(r, R_ROUND)
                    for i, kind in enumerate(R_KINDS):
                        hooks = {s: [lambda w=w: step(w, r) for w in ws] for s, ws in DVE_STEPS.get(i, {}).items()}
                        if i in (1, 7):
                            hooks.setdefault(4, []).append(lambda: n.add(TB=2))
                        if i in (2, 8):
                            hooks.setdefault(3, []).append(lambda: n.add(TB=2))
                        steps(hooks, 2 * i, 2)
                        if kind in ("q", "k"):
                            rotate(i % 2, i)
                        elif kind == "m2":
                            add_block(i % 2, i - 12)
                        n.unit(kind)
                    n.add(SB=3)
                    columns(bass.ds(r + 6, 1))
                n.leave(2)

            def between():
                mean_square()
                diagonals()

            mlp(0)
            between()
            retention()
            between()
            mlp(1)
            mean_square()
            dve.wait_ge(final_in, 16)
            for t in range(TT):
                dve.wait_ge(xn_done, t + 1)
                nc.vector.tensor_tensor(x[:, t, :], x[:, t, :], final_gain, ALU.mult).then_inc(o_ready, 1)

        @block.gpsimd
        def _(pool):
            n = Count()

            def clear():
                if n.n["GB"]:
                    pool.wait_ge(gate_mm, n.of("GB"))
                pool.wait_ge(col_mm, n.of("CS"))
                nc.gpsimd.memset(ada_acc[:], 0.0).then_inc(acc_clear, 1)

            def inverse_root():
                pool.wait_ge(ms_done, n.n["NO"] + 1)
                nc.gpsimd.tensor_tensor(rstd[:], meansq[:], minus_half[:], ALU.pow).then_inc(rstd_done, 1)
                n.add(NO=1)

            nc.gpsimd.memset(rows[:], 0.0).then_inc(rows_zero, 1)
            nc.gpsimd.memset(ada_acc[:], 0.0).then_inc(acc_clear, 1)
            nc.gpsimd.memset(ones[:], 1.0).then_inc(ones_set, 1)
            nc.gpsimd.memset(minus_half[:], -0.5).then_inc(half_set, 1)
            pool.wait_ge(half_set, 1)
            inverse_root()
            for seg in range(2):
                n.add(CS=1)
                clear()
            n.add(GB=4)
            clear()
            n.add(CS=1)
            clear()
            inverse_root()
            n.add(CS=1)
            clear()

            def mlp(layer):
                for first, trips, plan in MLP_PLAN[layer]:
                    what = plan[1]

                    for _ in range(trips):
                        if what == "now":
                            n.add(GB=4)
                            clear()
                        if what == "col":
                            n.add(CS=1)
                            clear()
                inverse_root()

            mlp(0)
            n.add(GB=4)
            clear()
            for _ in range(2):
                for hd in range(GROUP_HEADS):
                    pool.wait_ge(var_done, n.of("Y") + 1)
                    nc.gpsimd.tensor_tensor(y_rstd[:], y_var[:], minus_half[:], ALU.pow).then_inc(z_rstd, 1)
                    n.add(Y=1)
                n.add(CS=1)
                clear()
            inverse_root()
            mlp(1)


_INS = ["x", "c", "ada_w", "ada_b", "norm_g", "pool_w", "pool_scale", "ret_w_in", "ret_w_out", "mlp_w1", "mlp_w2",
        "final_g"]


def tables():
    ident = np.eye(P, dtype=np.float32)
    inv = np.float32(10000.0) ** (-np.arange(0, 2 * P, 2, dtype=np.float32) / np.float32(2 * P))
    ang = (np.arange(S, dtype=np.float32)[:, None] * inv[None, :]).astype(np.float64)

    def by_token(a):
        return np.ascontiguousarray(np.repeat(a, 2, axis=1).reshape(TT, P, 2 * P).transpose(1, 0, 2).astype(np.float32))

    log_g = np.log(1.0 - 2.0 ** (-5.0 - np.arange(HEADS)))
    j = np.arange(P, dtype=np.float64)
    diff = j[None, :] - j[:, None]
    decay = np.zeros((P, HEADS, S))
    for h in range(HEADS):
        decay[:, h, 0:P] = np.where(diff >= 0, np.exp(np.maximum(diff, 0.0) * log_g[h]), 0.0)
        decay[:, h, P:S] = np.exp((j[None, :] + 1.0) * log_g[h]) * np.exp((P - 1.0 - j[:, None]) * log_g[h])
    decay *= (2 * P) ** -0.5
    rcount = np.broadcast_to(1.0 / np.arange(1, 17), (P, 4, 16))
    return dict(ident=ident, cos=by_token(np.cos(ang)), sin=by_token(np.sin(ang)),
                decay=decay.astype(np.float32), rcount=np.ascontiguousarray(rcount.astype(np.float32)))


def kernel(**inputs):
    import concourse.bacc as _bacc
    from concourse.bass_utils import run_bass_kernel_spmd as _run

    nc = _bacc.Bacc("TRN2", target_bir_lowering=False, num_devices=1,
                     dynamic_dma_scratch_size=8192)
    arrays, args = {}, []
    data = {name: np.ascontiguousarray(inputs[name]) for name in _INS}
    data.update(tables())
    for name, a in data.items():
        arrays[f"in_{name}"] = a
        args.append(nc.dram_tensor(f"in_{name}", a.shape, mybir.dt.from_np(a.dtype), kind="ExternalInput").ap())
    out = nc.dram_tensor("out_0", (1, S, D), F32, kind="ExternalOutput").ap()
    program(nc, *args, out)
    r = _run(nc, [arrays], core_ids=[0])
    return r.results[0]["out_0"]
```

```python
from contextlib import ExitStack

import numpy as np

import concourse.bass as bass
from concourse import mybir

ALU = mybir.AluOpType
ACT = mybir.ActivationFunctionType
AX_X = mybir.AxisListType.X
F32 = mybir.dt.float32
F32R = mybir.dt.float32r

P = 128
D = 2048
S = 256
TT = S // P
KT = D // P
FF = 4 * D
NB = 512
CH = 8
CK = KT // CH
RING = 4
LEAD = RING
AW = 1024
SEG = KT * D // AW
HEADS = 8
GROUP_HEADS = 4
DV = 512
EPS = 1e-6
WINDOWS = (2, 4, 8, 16)
P_WIN = (1, 0, 0, 1)
M_UNITS = 8
R_UNITS = 16

UNIT = {
    "m1": dict(U=1, E=1, SQ=1),
    "m2": dict(U=1, E=1, XA=1),
    "q": dict(U=1, E=1, RO=1),
    "k": dict(U=1, E=1, RO=1),
    "g": dict(U=1, E=1),
    "v": dict(U=1, E=1),
}


class Count:

    NAMES = ("U", "E", "SQ", "XA", "RO", "TB", "TL", "SC", "Y", "AD", "AP", "SG", "RM", "TR", "TS", "CS", "GB", "NO", "HT", "SB")

    def __init__(self):
        self.n = {k: 0 for k in self.NAMES}
        self.reg, self.per = None, {}

    def add(self, **more):
        for k, v in more.items():
            self.n[k] += v

    def unit(self, kind):
        self.add(**UNIT[kind])

    def of(self, k):
        per = self.per.get(k, 0)
        return self.n[k] if self.reg is None or per == 0 else self.reg * per + self.n[k]

    def enter(self, reg, per):
        self.reg, self.per, self.kept = reg, per, dict(self.n)

    def leave(self, trips):
        for k in self.NAMES:
            seen = self.n[k] - self.kept[k]
            assert seen <= self.per.get(k, 0), (k, seen, self.per)
            self.n[k] = self.kept[k] + trips * self.per.get(k, 0)
        self.reg, self.per = None, {}


M_KINDS = ["m1"] * 4 + ["m2"] * 4
PAIR = ["q", "k", "g", "v", "g", "v"]
R_KINDS = PAIR * 2 + ["m2"] * 4

ADA_GATE_NOW = ([4, 6, 6, 6, 5, 5, 0, 0], "now")
ADA_COL = ([5, 5, 5, 5, 4, 4, 4, 0], "col")
ADA_GATE_KEPT = ([5, 5, 5, 5, 4, 4, 4, 0], "kept")
ADA_NONE = ([0] * 8, None)
ADA_RET = [3] * 2 + [2] * 13 + [0]
M_ROUND = dict(U=8, E=8, SQ=4, XA=4, TB=8, TL=8, SB=3)
R_ROUND = dict(U=16, E=20, XA=4, RO=4, TB=16, TL=8, SC=4, Y=4, AD=SEG, SG=1, RM=1, TR=1, TS=1, CS=1, SB=3)


def mlp_round(plan):
    spread, what = plan
    return dict(M_ROUND, AD=sum(spread), **(dict(SG=1, RM=1, TR=1, TS=1, CS=1) if what == "col" else {}))


MLP_PLAN = {
    0: [(0, 1, ADA_GATE_NOW), (1, 2, ADA_COL), (3, 1, ADA_GATE_KEPT)],
    1: [(0, 1, ADA_GATE_NOW), (1, 2, ADA_NONE), (3, 1, ADA_NONE)],
}

PE_STEPS = {1: {4: ["T rot"]}, 2: {3: ["T rot"]}, 3: {1: [("scores", 0)]}, 4: {3: [("weigh", 0)]},
            5: {1: [("scores", 1)], 3: ["T z"]},
            6: {3: [("weigh", 1)]}, 7: {2: ["T z"], 4: ["T rot"]}, 8: {3: ["T rot"]},
            9: {1: [("scores", 2)]}, 10: {3: [("weigh", 2)]}, 11: {1: [("scores", 3)], 3: ["T z"]},
            12: {0: [("weigh", 3)], 3: ["T z"]}}
ACT_STEPS = {1: {4: [("q",)]}, 2: {3: [("k",)]}, 4: {3: [("y", 0)]}, 5: {1: [("z", 0)], 3: [("a", 0)]},
             6: {3: [("y", 1)]}, 7: {0: [("z", 1)], 2: [("a", 1)], 4: [("q",)]}, 8: {3: [("k",)]},
             10: {3: [("y", 2)]}, 11: {1: [("z", 2)], 3: [("a", 2)]},
             12: {0: [("y", 3)], 1: [("z", 3)], 3: [("a", 3)]}}
DVE_STEPS = {3: {1: [("probs", 0)]}, 4: {3: [("norm", 0)]}, 5: {1: [("probs", 1)], 3: [("lo", 0)]},
             6: {3: [("norm", 1)]}, 7: {2: [("lo", 1)]},
             9: {1: [("probs", 2)]}, 10: {3: [("norm", 2)]}, 11: {1: [("probs", 3)], 3: [("lo", 2)]},
             12: {0: [("norm", 3)], 3: [("lo", 3)]}}


def program(nc, x_in, c_in, ada_w, ada_b, norm_g, pool_w, pool_scale, ret_w_in, ret_w_out, mlp_w1, mlp_w2,
            final_g, ident_in, cos_in, sin_in, decay_in, rcount_in, out):
    with ExitStack() as ctx:
        def sb(name, shape, dt=F32):
            return ctx.enter_context(nc.sbuf_tensor(name, shape, dt))

        def sem(name):
            return ctx.enter_context(nc.semaphore(name))

        raw = sb("raw", [P, RING, CK, NB])
        w_hi = sb("w_hi", [P, RING, CK, NB], F32R)
        w_lo = sb("w_lo", [P, RING, CK, NB], F32R)
        ada_raw = sb("ada_raw", [P, RING, AW])
        ada_acc = sb("ada_acc", [P, D])
        seg_row = sb("seg_row", [P, NB])
        bias_row = sb("bias_row", [P, NB])
        scale_row = sb("scale_row", [P, NB])
        col_rows = sb("col_rows", [P, P])
        x = sb("x", [P, TT, D])
        h_hi = sb("h_hi", [P, KT, S], F32R)
        h_lo = sb("h_lo", [P, KT, S], F32R)
        a_hi = sb("a_hi", [P, KT, S], F32R)
        a_lo = sb("a_lo", [P, KT, S], F32R)
        gate = sb("gate", [P, D])
        ev = sb("ev", [P, 2, TT, NB])
        ident = sb("ident", [P, P])
        ones = sb("ones", [P, P])
        diag = sb("diag", [P, TT, P])
        rows = sb("rows", [P, 2, P])
        norm_col = sb("norm_col", [P, 4, KT])
        mod_col = sb("mod_col", [P, 8, KT])
        gain_col = sb("gain_col", [P, 4, KT])
        cond = sb("cond", [P, KT])
        rcount = sb("rcount", [P, 4, 16])
        sq_junk = sb("sq_junk", [P, TT, NB], mybir.dt.bfloat16)
        ssq = sb("ssq", [P, TT, 4])
        ssum = sb("ssum", [P, TT])
        meansq = sb("meansq", [P, TT])
        rstd = sb("rstd", [P, TT])
        minus_half = sb("minus_half", [P, TT])
        y_stats = sb("y_stats", [P, TT, 6])
        y_mv = sb("y_mv", [P, TT, 2])
        y_var = sb("y_var", [P, TT])
        y_rstd = sb("y_rstd", [P, TT])
        scratch = sb("scratch", [P, 8192 + 384])
        h32 = scratch[:, 0:4096].rearrange("p (k t) -> p k t", k=KT)
        win = [scratch[:, 4096 + 1024 * i:5120 + 1024 * i].rearrange("p (k t) -> p k t", k=4) for i in range(2)]
        hbuf = [scratch[:, 512 * i:512 * (i + 1)].rearrange("p (k t) -> p k t", k=2) for i in range(2)]
        ybuf = scratch[:, 0:1024].rearrange("p (t n) -> p t n", t=TT)
        rot_a = scratch[:, 1024:1536]
        rot_b = scratch[:, 1536:2048]
        rot = scratch[:, 2048:3072].rearrange("p (t n) -> p t n", t=TT)
        qT = scratch[:, 3072:4096].rearrange("p (k t) -> p k t", k=4)
        kT = scratch[:, 4096:5120].rearrange("p (k t) -> p k t", k=4)
        decay = scratch[:, 5120:7168].rearrange("p (h t) -> p h t", h=HEADS)
        cos = scratch[:, 7168:7680].rearrange("p (t i) -> p t i", t=TT)
        sin = scratch[:, 7680:8192].rearrange("p (t i) -> p t i", t=TT)
        probs = scratch[:, 8192:8192 + 384]
        final_gain = scratch[:, 4096:6144]

        acc = [[ctx.enter_context(nc.psum_tensor(f"acc{p}{t}", [P, NB], F32)) for t in range(TT)] for p in range(2)]
        tb = [ctx.enter_context(nc.psum_tensor(f"tb{i}", [P, NB], F32)) for i in range(2)]
        mod_ps = ctx.enter_context(nc.psum_tensor("mod_ps", [P, NB], F32))
        score_ps = ctx.enter_context(nc.psum_tensor("score_ps", [P, NB], F32))

        raw_in = [sem(f"raw_in{i}") for i in range(RING)]
        ada_in = [sem(f"ada_in{i}") for i in range(RING)]
        x_loaded = sem("x_loaded")
        rows_in = sem("rows_loaded")
        const_in = sem("const_loaded")
        bias_in = sem("bias_row_loaded")
        ret_in = sem("ret_tables_loaded")
        scale_in = sem("layer_scale_loaded")
        final_in = sem("final_g_loaded")
        out_done = sem("out_done")
        rows_zero = sem("rows_zero")
        ones_set = sem("ones_set")
        half_set = sem("half_set")
        cond_rows = sem("cond_rows")
        setup_T = sem("setup_transposed")
        setup_col = sem("setup_columns")
        hi_ready = sem("hi_ready")
        lo_ready = sem("lo_ready")
        w_used = sem("w_used")
        evac = sem("evac_done")
        sq_done = sem("squared")
        tr_done = sem("tr_bank_filled")
        tevac = sem("tr_bank_evacuated")
        tlo = sem("tr_bank_split")
        mul_done = sem("gated")
        x_added = sem("x_added")
        ab_done = sem("rot_products")
        rot_done = sem("rotated")
        score_done = sem("scores")
        prob_done = sem("probs")
        y_ready = sem("y_summed")
        bn_done = sem("y_stats_done")
        mv_done = sem("y_mv_done")
        var_done = sem("y_var_done")
        z_rstd = sem("y_rstd_done")
        z_mul = sem("z_gated")
        z_done = sem("z_scaled")
        ada_done = sem("ada_done")
        ada_pe = sem("ada_rows_multiplied")
        row_mm = sem("row_summed")
        row_biased = sem("row_biased")
        row_ready = sem("seg_row_ready")
        col_rows_in = sem("col_rows_in")
        col_T = sem("col_transposed")
        col_used = sem("mod_col_ready")
        gate_in = sem("gate_in")
        gain_ready = sem("gain_ready")
        ssq_done = sem("ssq_done")
        ssum_done = sem("ssum_done")
        ms_done = sem("meansq_done")
        rstd_done = sem("rstd_done")
        diag_ready = sem("diag_ready")
        hhi_done = sem("h_hi_done")
        h_ready = sem("h_ready")
        pool_step = sem("pool_step")
        p_ready = sem("p_ready")
        p_hi = sem("p_hi")
        p_lo = sem("p_lo")
        xn_done = sem("x_normed")
        o_ready = sem("out_ready")

        block = ctx.enter_context(nc.Block())

        def rows_of(weights, chunk, col):
            return weights[chunk * CK * P:(chunk + 1) * CK * P, col].rearrange("(k p) n -> p k n", p=P)

        @block.sync
        def _(sp):
            n = Count()
            ada_flat = ada_w.rearrange("i s d (j k) -> (i s) d j k", j=3)

            def load_chunk(c, source):
                if n.reg is not None or CH * n.of("U") + c >= RING:
                    sp.wait_ge(lo_ready, n.of("U") * CH + (c - RING + 1))
                sp.dma_start(raw[:, c % RING], source).then_inc(raw_in[c % RING], 16)

            def load_ada(seg, a, shared=False):
                if shared:
                    if a % 2:
                        if n.n["AP"] >= 2:
                            sp.wait_ge(ada_pe, n.n["AP"] - 1)
                    elif n.n["AD"] >= 2:
                        sp.wait_ge(ada_done, n.n["AD"] - 1)
                elif n.reg is None and n.n["AD"] < n.n["AP"] + RING:
                    sp.wait_ge(ada_done, n.n["AP"])
                    sp.wait_ge(ada_pe, n.n["AP"])
                else:
                    sp.wait_ge(ada_done, n.of("AD") - (RING - 1))
                norm, part = (seg // 3, seg % 3) if isinstance(seg, int) else seg
                src = ada_flat[norm, (a % KT) * P:(a % KT + 1) * P, bass.ds(part, 1),
                               (a // KT) * AW:(a // KT + 1) * AW].rearrange("p j k -> p (j k)")
                sp.dma_start(ada_raw[:, a % RING], src).then_inc(ada_in[a % RING], 16)
                if shared and a % 2:
                    n.add(AP=1)
                else:
                    n.add(AD=1)

            def unit(kind, source, seg, a0, count):
                behind = {c: [] for c in range(CH)}
                for j in range(count):
                    step = next(s for s in range(CH) if count * (s + 1) // CH > j)
                    behind[min(CH - 1, step + 2)].append(a0 + j)
                for c in range(CH):
                    load_chunk(c, source(c))
                    for a in behind[c]:
                        load_ada(seg, a)
                n.unit(kind)

            def rows_of(weights, col):
                return lambda c: weights[c * CK * P:(c + 1) * CK * P, col].rearrange("(k p) n -> p k n", p=P)

            def group_rows_of(weights, g, block_):
                grouped = weights.rearrange("(g k p) n -> g p k n", k=KT, p=P)
                return lambda c: grouped[bass.ds(g, 1), :, c * CK:(c + 1) * CK,
                                         block_ * NB:(block_ + 1) * NB].rearrange("g p k n -> p (g k) n")

            sp.wait_ge(rows_zero, 1)
            sp.dma_start(rows[0:KT, 1, :], c_in.rearrange("b (k p) -> (b k) p", p=P)).then_inc(rows_in, 16)
            sp.dma_start(rows[0:64, 0, :], norm_g.rearrange("i s (k p) -> (i s k) p", p=P)).then_inc(rows_in, 16)
            sp.dma_start(ident[:], ident_in).then_inc(const_in, 16)
            sp.dma_start(rcount[:], rcount_in).then_inc(const_in, 16)
            for a in range(RING):
                load_ada(0, a, True)
            for t in range(TT):
                sp.dma_start(x[:, t, :], x_in[0, t * P:(t + 1) * P, :]).then_inc(x_loaded, 16)
            for a in range(RING, SEG):
                load_ada(0, a, True)
            for a in range(SEG):
                load_ada(1, a, True)
            pool_rows = rows_of(pool_w.rearrange("l g c n -> (l g c) n"), slice(0, NB))
            for c in range(RING):
                load_chunk(c, pool_rows(c))
            for a in range(SEG):
                load_ada(2, a, True)
            for a in range(SEG):
                load_ada(3, a, True)
                if a % 4 == 3 and a < 16:
                    load_chunk(RING + a // 4, pool_rows(RING + a // 4))
            for a in range(SEG):
                load_ada(4, a, True)
            n.add(U=1)

            def mlp(layer):
                for first, trips, plan in MLP_PLAN[layer]:
                    spread, what = plan
                    kept_seg = {(0, 0): 5, (0, 3): 8, (1, 0): 11}.get((layer, first))

                    def group(g, seg):
                        for u in range(M_UNITS):
                            if u < 4:
                                source = rows_of(mlp_w1[layer], bass.ds(g * (4 * NB) + u * NB, NB))
                            else:
                                source = group_rows_of(mlp_w2[layer], g, u - 4)
                            unit(M_KINDS[u], source, seg, sum(spread[:u]), spread[u])

                    if trips == 1:
                        group(first, kept_seg)
                    else:
                        with sp.Fori(0, trips) as r:
                            n.enter(r, mlp_round(plan))
                            group(r + first, (2, r))
                        n.leave(trips)

            def retention():
                with sp.Fori(0, 2) as r:
                    n.enter(r, R_ROUND)
                    for i, kind in enumerate(R_KINDS):
                        pair, w = i // 6, i % 6
                        if kind == "m2":
                            source = group_rows_of(ret_w_out[0], r, i - 12)
                        else:
                            if kind in "qk":
                                col = r * (2 * NB) + (D * (kind == "k") + pair * NB)
                            else:
                                col = r * (GROUP_HEADS * NB) + (2 * D + 2 * D * (kind == "g") +
                                                                (2 * pair + (w - 2) // 2) * NB)
                            source = rows_of(ret_w_in[0], bass.ds(col, NB))
                        unit(kind, source, (3, r), sum(ADA_RET[:i]), ADA_RET[i])
                n.leave(2)

            mlp(0)
            retention()
            mlp(1)
            for t in range(TT):
                sp.wait_ge(o_ready, t + 1)
                sp.dma_start(out[0, t * P:(t + 1) * P, :], x[:, t, :]).then_inc(out_done, 16)
            sp.wait_ge(out_done, 16 * TT)

        @block.tensor
        def _(pe):
            n = Count()

            def chunk(c, lhs_hi, lhs_lo, pair, first, last):
                for j in range(CK):
                    for t in range(TT):
                        tok = slice(t * P, (t + 1) * P)
                        for i, (l, w) in enumerate(((lhs_lo, w_hi), (lhs_hi, w_lo), (lhs_hi, w_hi))):
                            mm = nc.tensor.matmul(acc[pair][t][:], l[:, CK * c + j, tok], w[:, c % RING, j, :],
                                                  start=first and j == 0 and i == 0,
                                                  stop=last and j == CK - 1 and i == 2)
                mm.then_inc(w_used, 1)

            def unit(kind, pair, hooks, lhs, ready):
                for c in range(CH):
                    pe.wait_ge(lo_ready, n.of("U") * CH + (c + 1))
                    ready(c)
                    if c == 0:
                        pe.wait_ge(evac, (n.of("E") - 1) * TT)
                    chunk(c, *lhs, pair, c == 0, c == CH - 1)
                    for hook in hooks.get(c, []):
                        hook()
                n.unit(kind)

            def transposes(source, split):
                for b in range(2):
                    pe.wait_ge(tevac, n.of("TB") + (b - 1))
                    pe.wait_ge(tlo, n.of("TL"))
                    for j in range(2):
                        for t in range(TT):
                            m = 2 * b + j
                            tr = nc.tensor.transpose(tb[b][:, j * S + t * P:j * S + (t + 1) * P],
                                                     source(t)[:, m * P:(m + 1) * P], ident[:])
                    tr.then_inc(tr_done, 1)
                n.add(TB=2, TL=2 if split else 0)

            def row_blocks(bank, b0, b1, start):
                for b in range(b0, b1):
                    mm = nc.tensor.matmul(bank[32 * b:32 * b + 32, :], ones[:, 0:32],
                                          ada_acc[:, b * NB:(b + 1) * NB], start=start, stop=True)
                mm.then_inc(row_mm, 1)
                n.add(RM=1)

            def shared_rows(seg, a0, a1):
                bank = (mod_ps, score_ps)[seg % 2]
                for a in range(a0 + 1, a1, 2):
                    k, half = a % KT, a // KT
                    if a == 1 and seg == 4:
                        pe.wait_ge(row_ready, 3)
                    elif a == 1 and seg >= 2:
                        pe.wait_ge(col_used, seg - 1)
                    pe.wait_ge(ada_in[a % RING], (seg * (SEG // RING) + a // RING + 1) * 16)
                    for b in (2 * half, 2 * half + 1):
                        mm = nc.tensor.matmul(bank[32 * b:32 * b + 32, :], cond[:, k:k + 1].to_broadcast([P, 32]),
                                              ada_raw[:, a % RING, b % 2 * NB:(b % 2 + 1) * NB], start=k == 1,
                                              stop=False)
                    mm.then_inc(ada_pe, 1)
                    n.add(AP=1)
                    if k == KT - 1:
                        n.add(AD=CH)
                        pe.wait_ge(ada_done, n.n["AD"])
                        row_blocks(bank, 2 * half, 2 * half + 2, False)

            def row_sum(b0, b1, chunks):
                pe.wait_ge(ada_done, chunks)
                pe.wait_ge(row_ready, n.of("TR"))
                pe.wait_ge(col_used, n.of("CS"))
                row_blocks(mod_ps, b0, b1, True)
                n.add(TR=1)

            def column(bank):
                pe.wait_ge(col_rows_in, 16 * (n.of("CS") + 1))
                nc.tensor.transpose(bank[:, 0:P], col_rows[:], ident[:]).then_inc(col_T, 1)
                n.add(CS=1)

            def norm_fill(f):
                if n.of("TB") >= 2:
                    pe.wait_ge(tevac, n.of("TB") - 1)
                if f < 2 and n.of("TL"):
                    pe.wait_ge(tlo, n.of("TL"))
                for j in range(2):
                    for t in range(TT):
                        k = 2 * f + j
                        tr = nc.tensor.matmul(tb[f % 2][:, j * S + t * P:j * S + (t + 1) * P],
                                              x[:, t, k * P:(k + 1) * P], diag[:, t, :], start=True, stop=True)
                tr.then_inc(tr_done, 1)
                n.add(TB=1)

            def norm(banks=KT // 2):
                pe.wait_ge(diag_ready, n.of("NO") + 1)
                for f in range(banks):
                    norm_fill(f)
                n.add(NO=1)

            pe.wait_ge(const_in, 32)
            pe.wait_ge(cond_rows, 1)
            for i in range(2):
                tr = nc.tensor.transpose(tb[0][:, i * P:(i + 1) * P], rows[:, i, :], ident[:])
            tr.then_inc(setup_T, 1)
            pe.wait_ge(ones_set, 1)
            pe.wait_ge(setup_col, 1)
            shared_rows(0, 0, SEG)
            shared_rows(1, 0, 16)
            column(mod_ps)
            shared_rows(1, 16, SEG)
            shared_rows(2, 0, 8)
            column(score_ps)
            norm(2)
            for f in range(2, KT // 2):
                shared_rows(2, 4 + 2 * f, 6 + 2 * f)
                norm_fill(f)
            shared_rows(2, 20, SEG)
            for gi in range(4):
                shared_rows(3, gi * CH, (gi + 1) * CH)
                for c in (2 * gi, 2 * gi + 1):
                    pe.wait_ge(lo_ready, c + 1)
                    if c == 2 * gi:
                        pe.wait_ge(p_lo, gi + 1)
                        if gi >= 2:
                            pe.wait_ge(evac, (gi - 1) * TT)
                    chunk(c, a_hi, a_lo, gi % 2, c == 2 * gi, c == 2 * gi + 1)
            n.add(U=1, E=4)
            shared_rows(4, 0, 12)
            column(score_ps)
            shared_rows(4, 12, SEG)
            norm(2)
            column(mod_ps)
            n.add(TR=5)

            def ready_h(c):
                pe.wait_ge(h_ready, n.n["HT"] - CH + c + 1)

            def mlp(layer):
                if layer:
                    norm(2)
                n.add(HT=CH)
                for first, trips, plan in MLP_PLAN[layer]:
                    spread, what = plan

                    def group():
                        split0, ada0 = n.of("TL"), n.of("AD")
                        for u in range(M_UNITS):
                            hooks = {}
                            if first == 0 and u == 0:
                                hooks = {f - 2: [lambda f=f: norm_fill(f)] for f in range(2, KT // 2)}
                            if what == "now" and u in (4, 6):
                                b = u - 4
                                hooks[0] = [lambda b=b: row_sum(b, b + 2, ada0 + SEG // 4 * (b + 2))]
                            elif what and what != "now" and u == 7:
                                hooks[0] = [lambda: row_sum(0, 4, n.of("AD"))]
                            if 1 <= u <= 4:
                                def transpose_squares(pair=(u - 1) % 2):
                                    pe.wait_ge(sq_done, n.of("SQ") * TT)
                                    transposes(lambda t: ev[:, pair, t, :], True)
                                hooks[2] = [transpose_squares]
                            if u < 4:
                                unit("m1", u % 2, hooks, (h_hi, h_lo), ready_h)
                            else:
                                unit("m2", u % 2, hooks, (a_hi, a_lo), lambda c: pe.wait_ge(tlo, split0 + (c + 1)))
                            n.add(AD=spread[u])
                        if what == "col":
                            column(mod_ps)

                    if trips == 1:
                        group()
                    else:
                        with pe.Fori(0, trips) as r:
                            n.enter(r, mlp_round(plan))
                            group()
                        n.leave(trips)

            def scores(hd):
                pe.wait_ge(tevac, n.of("TB"))
                if hd:
                    pe.wait_ge(prob_done, n.of("SC"))
                w = (hd % 2) * 2
                for part, q0 in ((0, 0), (1, P)):
                    for j in range(2):
                        mm = nc.tensor.matmul(score_ps[:, part * S:part * S + S - q0],
                                              kT[:, w + j, part * P:(part + 1) * P], qT[:, w + j, q0:S],
                                              start=j == 0, stop=j == 1)
                mm.then_inc(score_done, 1)
                n.add(SC=1)

            def weigh(pair):
                pe.wait_ge(prob_done, n.of("Y") + 1)
                pe.wait_ge(evac, n.of("E") * TT)
                nc.tensor.matmul(acc[pair][0][:], probs[:, 0:P], ev[:, 1, 0, :], start=True, stop=True)
                nc.tensor.matmul(acc[pair][1][:], probs[:, P:S], ev[:, 1, 0, :], start=True, stop=False)
                nc.tensor.matmul(acc[pair][1][:], probs[:, S:S + P], ev[:, 1, 1, :], start=False,
                                 stop=True).then_inc(y_ready, 1)
                n.add(E=1, Y=1)

            def transpose_rotated():
                pe.wait_ge(rot_done, n.of("RO") * TT)
                transposes(lambda t: rot[:, t, :], False)

            def transpose_z():
                pe.wait_ge(z_done, n.of("Y"))
                transposes(lambda t: ybuf[:, t, :], True)

            def retention():
                norm()
                n.add(HT=CH)
                with pe.Fori(0, 2) as r:
                    n.enter(r, R_ROUND)
                    split0 = n.of("TL")
                    for i, kind in enumerate(R_KINDS):
                        hooks = {}
                        for c, steps in PE_STEPS.get(i, {}).items():
                            hooks[c] = [transpose_rotated if s == "T rot" else transpose_z if s == "T z" else
                                        (lambda s=s, i=i: scores(s[1]) if s[0] == "scores" else weigh((i - 1) % 2))
                                        for s in steps]
                        if i == R_UNITS - 1:
                            hooks[0] = [lambda: row_sum(0, 4, n.of("AD"))]
                        if kind == "m2":
                            unit(kind, i % 2, hooks, (a_hi, a_lo), lambda c: pe.wait_ge(tlo, split0 + (c + 1)))
                        else:
                            unit(kind, i % 2, hooks, (h_hi, h_lo), ready_h)
                        n.add(AD=ADA_RET[i])
                    column(mod_ps)
                n.leave(2)

            mlp(0)
            retention()
            mlp(1)

        @block.scalar
        def _(act):
            n = Count()

            def hi(c, ahead=0):
                u = n.of("U") + ahead
                if c % 1 == 0:
                    act.wait_ge(raw_in[c % RING], (u * 2 + (c // RING + 1)) * 16)
                if not (n.reg is None and u * CH + c < RING):
                    act.wait_ge(w_used, u * CH + (c - RING + 1))
                nc.scalar.activation(w_hi[:, c % RING], raw[:, c % RING], ACT.Copy).then_inc(hi_ready, 1)

            def steps(hooks):
                for s in range(CH):
                    if s < CH - LEAD:
                        hi(s + LEAD)
                    elif not (ending[0]):
                        hi(s + LEAD - CH, 1)
                    for hook in hooks.get(s, []):
                        hook()

            ending = [False]

            def evacuate(pair, func, target, counts=True):
                for t in range(TT):
                    nc.scalar.activation(target[:, t, :], acc[pair][t][:], func).then_inc(evac, 1)
                n.add(E=1)

            def evacuate_T(targets, b):
                act.wait_ge(tr_done, n.of("TB") + 1)
                nc.scalar.activation(targets, tb[b][:].rearrange("p (k t) -> p k t", k=2), ACT.Copy).then_inc(tevac, 1)
                n.add(TB=1)

            def squares(block_):
                for t in range(TT):
                    if n.reg is not None or n.of("SB"):
                        act.wait_ge(ssq_done, (n.of("SB") - 1) * TT + t + 1)
                    nc.scalar.activation(sq_junk[:, t, :], x[:, t, block_ * NB:(block_ + 1) * NB], ACT.Square,
                                         accum_out=ssq[:, t, block_:block_ + 1]).then_inc(ssq_done, 1)
                n.add(SB=1)

            def unit_done():
                act.wait_ge(w_used, (n.of("U") + 1) * CH)

            def norm_evac(f, target):
                act.wait_ge(tr_done, n.of("TB") + 1)
                k0 = n.n["NO"]
                for j in range(2):
                    k = 2 * f + j
                    h = nc.scalar.activation(target[:, j, :], tb[f % 2][:, j * S:(j + 1) * S], ACT.Identity,
                                             bias=mod_col[:, 2 * k0, k:k + 1], scale=gain_col[:, k0, k:k + 1])
                h.then_inc(tevac, 1)
                n.add(TB=1)
                if f == KT // 2 - 1:
                    n.add(NO=1)

            def norm_bank(f):
                if f == 0:
                    act.wait_ge(gain_ready, n.n["NO"] + 1)
                if f >= 2:
                    act.wait_ge(h_ready, n.n["HT"] + f - 1)
                norm_evac(f, hbuf[f % 2])
                if f == KT // 2 - 1:
                    n.add(HT=CH)

            def by_block(row):
                return row.rearrange("(b o n) -> b o n", b=4, o=1).to_broadcast([4, 32, NB])

            def load_bias(norm_, part):
                row = ada_b.rearrange("i s (j k) -> (i s) j k", j=3)[norm_, bass.ds(part, 1), :]
                act.dma_start(bias_row[:], by_block(row.rearrange("j k -> (j k)"))).then_inc(bias_in, 16)

            def send_column():
                act.wait_ge(row_ready, n.of("TR") + 1)
                if n.n["CS"]:
                    act.wait_ge(col_T, n.of("CS"))
                else:
                    act.wait_ge(rows_zero, 1)
                act.dma_start(col_rows[0:KT, :], seg_row[0:P:32, :].rearrange("p (m c) -> p m c", m=4)).then_inc(
                    col_rows_in, 16)
                n.add(TR=1, CS=1)

            def send_gate(b0, b1):
                act.wait_ge(row_ready, n.of("TR") + 1)
                if n.n["XA"]:
                    act.wait_ge(x_added, n.n["XA"] * TT)
                for b in range(b0, b1):
                    row = seg_row[32 * b:32 * b + 1, :].rearrange("p (o n) -> p o n", o=1).to_broadcast([1, P, NB])
                    act.dma_start(gate[:, b * NB:(b + 1) * NB], row).then_inc(gate_in, 16)
                n.add(TR=1)

            load_bias(0, 0)
            act.dma_start(scale_row[:], by_block(pool_scale.rearrange("a k -> (a k)"))).then_inc(scale_in, 16)
            act.wait_ge(rows_in, 16 * 2)
            nc.scalar.activation(rows[:, 1, :], rows[:, 1, :], ACT.Silu).then_inc(cond_rows, 1)
            act.wait_ge(x_loaded, 16 * TT)
            for b in range(4):
                squares(b)
            for seg in range(2):
                send_column()
                load_bias(0, seg + 1)
            act.wait_ge(gain_ready, 1)
            for f in range(4):
                norm_evac(f, h32[:, 2 * f:2 * f + 2, :])
            for gi in range(4):
                act.wait_ge(p_ready, gi + 1)
                nc.scalar.activation(a_hi[:, 4 * gi:4 * gi + 4, :], win[P_WIN[gi]], ACT.Copy).then_inc(p_hi, 1)
                if gi < 2:
                    for f in (4 + 2 * gi, 5 + 2 * gi):
                        norm_evac(f, h32[:, 2 * f:2 * f + 2, :])
                    hi(2 * gi)
                    hi(2 * gi + 1)
            send_gate(0, 4)
            load_bias(1, 0)
            for gi in range(4):
                if gi < 2:
                    hi(LEAD + 2 * gi)
                    hi(LEAD + 2 * gi + 1)
                act.wait_ge(w_used, 2 * gi + 2)
                if gi >= 2:
                    act.wait_ge(x_added, (gi - 1) * TT)
                evacuate(gi % 2, ACT.Copy, ev[:, gi % 2])
            act.wait_ge(x_added, 4 * TT)
            n.add(XA=4)
            for b in range(4):
                squares(b)
            send_column()
            load_bias(1, 1)
            send_column()
            load_bias(1, 2)
            for c in range(LEAD):
                hi(c, 1)
            n.add(U=1)

            def mlp(layer):
                for f in range(3):
                    norm_bank(f)
                for first, trips, plan in MLP_PLAN[layer]:
                    what = plan[1]

                    def group(end, r=None):
                        for u in range(M_UNITS):
                            hooks = {}
                            if first == 0 and u == 0:
                                hooks = {f - 3: [lambda f=f: norm_bank(f)] for f in range(3, KT // 2)}
                            if 1 <= u <= 4:
                                def upper(u=u):
                                    for b in range(2):
                                        k = 4 * (u - 1) + 2 * b
                                        evacuate_T(a_hi[:, k:k + 2, :], b)
                                hooks[2] = [upper]
                            if u > 4:
                                def block_squares(u=u):
                                    act.wait_ge(x_added, n.of("XA") * TT)
                                    squares(u - 5)
                                hooks[2] = [block_squares]
                            if what == "now" and u in (4, 6):
                                hooks.setdefault(4, []).append(lambda b=u - 4: send_gate(b, b + 2))
                                if u == 6 and layer == 0:
                                    hooks[4].append(lambda: load_bias(2, 0))
                            elif what == "col" and u == 7:
                                hooks[4] = [send_column, lambda: load_bias(2, r + 1)]
                            ending[0] = end and u == M_UNITS - 1
                            steps(hooks)
                            unit_done()
                            if u < 4:
                                if u < 2:
                                    act.wait_ge(x_added, (n.of("XA") - (1 - u)) * TT)
                                evacuate(u % 2, ACT.Relu, ev[:, u % 2])
                                for t in range(TT):
                                    act.wait_ge(evac, (n.of("E") - 1) * TT + t + 1)
                                    nc.scalar.activation(ev[:, u % 2, t, :], ev[:, u % 2, t, :],
                                                         ACT.Square).then_inc(sq_done, 1)
                            else:
                                if u >= 6:
                                    act.wait_ge(x_added, (n.of("XA") - 1) * TT)
                                evacuate(u % 2, ACT.Copy, ev[:, u % 2])
                            n.unit(M_KINDS[u])
                            n.add(E=-1)

                    if trips == 1:
                        group(layer == 1 and first == 3)
                    else:
                        with act.Fori(0, trips) as r:
                            n.enter(r, mlp_round(plan))
                            group(False, r)
                        n.leave(trips)

            def between():
                act.wait_ge(x_added, n.of("XA") * TT)
                squares(3)

            def retention():
                act.dma_start(decay, decay_in).then_inc(ret_in, 16)
                act.dma_start(cos, cos_in).then_inc(ret_in, 16)
                act.dma_start(sin, sin_in).then_inc(ret_in, 16)
                for f in range(KT // 2):
                    norm_bank(f)
                with act.Fori(0, 2) as r:
                    n.enter(r, R_ROUND)
                    for i, kind in enumerate(R_KINDS):
                        hooks = {s: [lambda what=w, i=i: step(what, i) for w in ws]
                                 for s, ws in ACT_STEPS.get(i, {}).items()}
                        if i > 12:
                            def block_squares(i=i):
                                act.wait_ge(x_added, n.of("XA") * TT)
                                squares(i - 13)
                            hooks[2] = [block_squares]
                        if i == R_UNITS - 1:
                            hooks[4] = [send_column, lambda: load_bias(3, r + 1)]
                        steps(hooks)
                        unit_done()
                        if i < 2:
                            act.wait_ge(x_added, (n.of("XA") - (1 - i)) * TT)
                        elif i in (2, 8):
                            act.wait_ge(rot_done, (n.of("RO") - 1) * TT)
                        elif i in (3, 9):
                            act.wait_ge(rot_done, n.of("RO") * TT)
                        elif i in (4, 6, 10, 12):
                            act.wait_ge(z_mul, n.of("Y") * TT)
                        elif i >= 14:
                            act.wait_ge(x_added, (n.of("XA") - 1) * TT)
                        evacuate(i % 2, ACT.Silu if kind == "g" else ACT.Copy, ev[:, i % 2])
                        n.unit(kind)
                        n.add(E=-1)
                n.leave(2)

            def step(what, i):
                if what[0] in ("q", "k"):
                    target = qT if what[0] == "q" else kT
                    for b in range(2):
                        evacuate_T(target[:, 2 * b:2 * b + 2, :], b)
                elif what[0] == "a":
                    for b in range(2):
                        k = 4 * what[1] + 2 * b
                        evacuate_T(a_hi[:, k:k + 2, :], b)
                elif what[0] == "y":
                    act.wait_ge(y_ready, n.of("Y") + 1)
                    evacuate((i - 1) % 2, ACT.Copy, ybuf)
                    n.add(Y=1)
                else:
                    act.wait_ge(z_mul, n.of("Y") * TT)
                    act.wait_ge(z_rstd, n.of("Y"))
                    for t in range(TT):
                        z = nc.scalar.activation(ybuf[:, t, :], ybuf[:, t, :], ACT.Copy, scale=y_rstd[:, t:t + 1])
                    z.then_inc(z_done, 1)

            mlp(0)
            between()
            send_gate(0, 4)
            load_bias(3, 0)
            retention()
            between()
            act.dma_start(final_gain, final_g.rearrange("(a n) -> a n", a=1).to_broadcast([P, D])).then_inc(final_in, 16)
            mlp(1)
            between()
            act.wait_ge(rstd_done, 5)
            for t in range(TT):
                nc.scalar.activation(x[:, t, :], x[:, t, :], ACT.Copy, scale=rstd[:, t:t + 1]).then_inc(xn_done, 1)

        @block.vector
        def _(dve):
            n = Count()

            def lo(c, ahead=0):
                dve.wait_ge(hi_ready, (n.of("U") + ahead) * CH + (c + 1))
                nc.vector.tensor_tensor(w_lo[:, c % RING], raw[:, c % RING], w_hi[:, c % RING].bitcast(F32),
                                        ALU.subtract).then_inc(lo_ready, 1)

            def ada(a, shared=False):
                k, half = a % KT, a // KT
                if k:
                    dve.wait_ge(ada_done, n.of("AD"))
                elif shared and n.n["SG"]:
                    dve.wait_ge(row_mm, 2 * n.n["SG"] + half - 1)
                dve.wait_ge(ada_in[a % RING], (ada_round() + (a // RING + 1)) * 16)
                part = ada_acc[:, half * AW:(half + 1) * AW]
                if k:
                    nc.vector.scalar_tensor_tensor(out=part, in0=ada_raw[:, a % RING], scalar=cond[:, k:k + 1],
                                                   in1=part, op0=ALU.mult, op1=ALU.add).then_inc(ada_done, 1)
                else:
                    nc.vector.tensor_scalar(part, ada_raw[:, a % RING], cond[:, k:k + 1], None,
                                            ALU.mult).then_inc(ada_done, 1)
                n.add(AD=1)
                if a == SEG - (2 if shared else 1):
                    n.add(SG=1)

            def ada_even(a0, a1):
                for a in range(a0, a1, 2):
                    ada(a, True)

            def ada_round():
                return n.of("SG") * (SEG // RING)

            def steps(hooks, a0, count, end=False):
                done = 0
                for s in range(CH):
                    if s < CH - LEAD:
                        lo(s + LEAD)
                    elif not end:
                        lo(s + LEAD - CH, 1)
                    while done < count * (s + 1) // CH:
                        ada(a0 + done)
                        done += 1
                    for hook in hooks.get(s, []):
                        hook()

            def take_rows(b0, b1, layer_scale=False):
                part = slice(32 * b0, 32 * b1)
                dve.wait_ge(row_mm, n.of("RM") + 1)
                dve.wait_ge(bias_in, 16 * (n.of("TS") + 1))
                if n.n["CS"]:
                    dve.wait_ge(col_rows_in, 16 * n.of("CS"))
                if n.n["GB"]:
                    dve.wait_ge(gate_in, 16 * n.of("GB"))
                row = nc.vector.tensor_tensor(seg_row[part, :], (score_ps if n.n["TS"] in (1, 3) else mod_ps)[part, :],
                                              bias_row[part, :], ALU.add)
                if layer_scale:
                    row.then_inc(row_biased, 1)
                    dve.wait_ge(scale_in, 16)
                    dve.wait_ge(row_biased, 1)
                    row = nc.vector.tensor_tensor(seg_row[:], seg_row[:], scale_row[:], ALU.mult)
                row.then_inc(row_ready, 1)
                n.add(RM=1, TR=1)
                if b1 == 4:
                    n.add(TS=1)

            def take_column(index, bank=mod_ps):
                dve.wait_ge(col_T, n.of("CS"))
                nc.vector.tensor_copy(mod_col[:, index, :].rearrange("p s k -> p (s k)"),
                                      bank[:, 0:KT]).then_inc(col_used, 1)

            def add_block(p, b):
                blk = slice(b * NB, (b + 1) * NB)
                for t in range(TT):
                    dve.wait_ge(evac, n.of("E") * TT + (t + 1))
                    nc.vector.tensor_tensor(ev[:, p, t, :], ev[:, p, t, :], gate[:, blk],
                                            ALU.mult).then_inc(mul_done, 1)
                for t in range(TT):
                    dve.wait_ge(mul_done, n.of("XA") * TT + (t + 1))
                    nc.vector.tensor_tensor(x[:, t, blk], x[:, t, blk], ev[:, p, t, :], ALU.add).then_inc(x_added, 1)

            def lower_T(k, b):
                dve.wait_ge(tevac, n.of("TB") + 1)
                nc.vector.tensor_tensor(a_lo[:, k:k + 2, :], tb[b][:].rearrange("p (k t) -> p k t", k=2),
                                        a_hi[:, k:k + 2, :].bitcast(F32), ALU.subtract).then_inc(tlo, 1)
                n.add(TB=1)

            def mean_square():
                m = n.n["NO"]
                n.add(SB=4 if m < 2 else 1)
                dve.wait_ge(ssq_done, n.n["SB"] * TT)
                nc.vector.tensor_reduce(ssum[:], ssq[:], AX_X, ALU.add).then_inc(ssum_done, 1)
                dve.wait_ge(ssum_done, m + 1)
                nc.vector.tensor_scalar(meansq[:], ssum[:], 1.0 / D, EPS, ALU.mult, ALU.add).then_inc(ms_done, 1)

            def diagonals():
                m = n.n["NO"]
                dve.wait_ge(rstd_done, m + 1)
                for t in range(TT):
                    d = nc.vector.tensor_scalar(diag[:, t, :], ident[:], rstd[:, t:t + 1], None, ALU.mult)
                d.then_inc(diag_ready, 1)

            def gains():
                m = n.n["NO"]
                dve.wait_ge(col_used, 2 * (m + 1))
                nc.vector.scalar_tensor_tensor(out=gain_col[:, m, :], in0=mod_col[:, 2 * m + 1, :], scalar=1.0,
                                               in1=norm_col[:, m, :], op0=ALU.add,
                                               op1=ALU.mult).then_inc(gain_ready, 1)
                n.add(NO=1)

            def split_h(f):
                own = n.n["HT"] + f + 1
                dve.wait_ge(tevac, n.of("TB") + 1)
                n.add(TB=1)
                nc.vector.tensor_copy(h_hi[:, 2 * f:2 * f + 2, :], hbuf[f % 2]).then_inc(hhi_done, 1)
                dve.wait_ge(hhi_done, own)
                nc.vector.tensor_tensor(h_lo[:, 2 * f:2 * f + 2, :], hbuf[f % 2],
                                        h_hi[:, 2 * f:2 * f + 2, :].bitcast(F32), ALU.subtract).then_inc(h_ready, 1)
                if f == KT // 2 - 1:
                    n.add(HT=CH)

            dve.wait_ge(setup_T, 1)
            nc.vector.tensor_copy(norm_col[:].rearrange("p s k -> p (s k)"), tb[0][:, 0:4 * KT])
            nc.vector.tensor_copy(cond[:], tb[0][:, P:P + KT]).then_inc(setup_col, 1)
            dve.wait_ge(setup_col, 1)

            def take_shared(layer_scale=False):
                n.add(RM=1)
                take_rows(0, 4, layer_scale)

            ada_even(0, 16)
            mean_square()
            ada_even(16, 24)
            diagonals()
            ada_even(24, SEG)
            ada_even(0, 8)
            take_shared()
            n.add(CS=1)
            ada_even(8, 16)
            take_column(slice(0, 1), mod_ps)
            ada_even(16, SEG)
            ada_even(0, 4)
            take_shared()
            n.add(CS=1)
            ada_even(4, 8)
            take_column(slice(1, 2), score_ps)
            gains()
            ada_even(8, 12)
            n.add(TB=CH)

            pool_count = [0]
            even_chunks = iter(list(range(12, SEG, 2)) + list(range(0, 24, 2)))

            def pool_op(ins, behind=1):
                ins.then_inc(pool_step, 1)
                pool_count[0] += 1
                for _ in range(behind):
                    ada(next(even_chunks), True)

            def own():
                dve.wait_ge(pool_step, pool_count[0])

            def pooled_lo(gi):
                dve.wait_ge(p_hi, gi + 1)
                nc.vector.tensor_tensor(a_lo[:, 4 * gi:4 * gi + 4, :], win[P_WIN[gi]],
                                        a_hi[:, 4 * gi:4 * gi + 4, :].bitcast(F32), ALU.subtract).then_inc(p_lo, 1)

            for gi, w in enumerate(WINDOWS):
                dve.wait_ge(tevac, 2 * gi + 2)
                h = h32[:, 4 * gi:4 * gi + 4, :]
                at = 1 - P_WIN[gi - 1] if gi else 0
                cur, s = h, 1
                while s < w:
                    dst = win[at]
                    if s > 1:
                        own()
                    pool_op(nc.vector.tensor_tensor(dst[:, :, s:], cur[:, :, s:], cur[:, :, :S - s], ALU.add), 1)
                    pool_op(nc.vector.tensor_copy(dst[:, :, :s], cur[:, :, :s]), 0)
                    cur, at = dst, 1 - at
                    if gi and s == 1:
                        pooled_lo(gi - 1)
                        dve.wait_ge(p_lo, gi)
                    s = 2 * s
                p = win[at]
                assert at == P_WIN[gi]
                own()
                pool_op(nc.vector.scalar_tensor_tensor(out=p, in0=cur, scalar=1.0 / w, in1=h, op0=ALU.mult,
                                                       op1=ALU.subtract))
                own()
                pool_op(nc.vector.tensor_tensor(p[:, :, :w], cur[:, :, :w], rcount[:, :, :w], ALU.mult), 1)
                own()
                nc.vector.tensor_tensor(p[:, :, :w], p[:, :, :w], h[:, :, :w], ALU.subtract).then_inc(p_ready, 1)
                ada(next(even_chunks), True)
                if gi in (1, 2):
                    lo(2 * gi - 2)
                    lo(2 * gi - 1)
            pooled_lo(3)
            for a in even_chunks:
                ada(a, True)
            take_shared(True)
            n.add(GB=4)
            for c in range(LEAD, CH):
                a = 24 + 2 * (c - LEAD)
                ada_even(a, a + 2)
                lo(c)
            dve.wait_ge(gate_in, 16 * 4)
            for gi in range(4):
                add_block(gi % 2, gi)
                n.add(E=1, XA=1)
                a = 2 * gi
                ada_even(a, a + 2)
            mean_square()
            take_shared()
            n.add(CS=1)
            ada_even(8, 12)
            diagonals()
            take_column(slice(2, 3), score_ps)
            ada_even(12, SEG)
            take_shared()
            n.add(CS=1)
            for c in range(LEAD):
                lo(c, 1)
            take_column(slice(3, 4), mod_ps)
            n.add(U=1)

            def mlp(layer):
                gains()
                for f in range(3):
                    split_h(f)
                for first, trips, plan in MLP_PLAN[layer]:
                    spread, what = plan

                    def group(r, end):
                        for u in range(M_UNITS):
                            hooks = {}
                            if first == 0 and u == 0:
                                hooks = {f - 3: [lambda f=f: split_h(f)] for f in range(3, KT // 2)}
                            if 1 <= u <= 4:
                                def lower(u=u):
                                    for b in range(2):
                                        lower_T(4 * (u - 1) + 2 * b, b)
                                hooks[2] = [lower]
                            if what == "now" and u in (4, 6):
                                def take_gate(b=u - 4):
                                    take_rows(b, b + 2)
                                    n.add(GB=2)
                                hooks.setdefault(2, []).append(take_gate)
                            elif what and what != "now" and u == 7:
                                hooks[2] = [lambda: take_rows(0, 4)]
                            steps(hooks, sum(spread[:u]), spread[u], end and u == M_UNITS - 1)
                            if u >= 4:
                                if what == "now":
                                    dve.wait_ge(gate_in, 16 * n.of("GB"))
                                add_block(u % 2, u - 4)
                            n.unit(M_KINDS[u])
                        n.add(SB=3)
                        if what == "col":
                            n.add(CS=1)
                            take_column(bass.ds(r + 4, 1))
                        elif what == "kept":
                            n.add(GB=4)

                    if trips == 1:
                        group(0, layer == 1 and first == 3)
                    else:
                        with dve.Fori(0, trips) as r:
                            n.enter(r, mlp_round(plan))
                            group(r, False)
                        n.leave(trips)

            def rotate(p, i):
                for t in range(TT):
                    src = ev[:, p, t, :].rearrange("p (h i) -> p h i", h=2)
                    dve.wait_ge(evac, n.of("E") * TT + (t + 1))
                    a3 = rot_a.rearrange("p (h i) -> p h i", h=2)
                    b3 = rot_b.rearrange("p (h i) -> p h i", h=2)
                    if t:
                        dve.wait_ge(rot_done, n.of("RO") * TT + t)
                    nc.vector.tensor_tensor(a3, src, cos[:, t:t + 1, :].to_broadcast([P, 2, 2 * P]), ALU.mult)
                    nc.vector.tensor_tensor(b3, src, sin[:, t:t + 1, :].to_broadcast([P, 2, 2 * P]),
                                            ALU.mult).then_inc(ab_done, 1)
                    dve.wait_ge(ab_done, n.of("RO") * TT + (t + 1))
                    a4 = rot_a.rearrange("p (h i two) -> p h i two", h=2, two=2)
                    b4 = rot_b.rearrange("p (h i two) -> p h i two", h=2, two=2)
                    o4 = rot[:, t, :].rearrange("p (h two i) -> p h two i", h=2, two=2)
                    nc.vector.tensor_tensor(o4[:, :, 0, :], a4[:, :, :, 0], b4[:, :, :, 1], ALU.subtract)
                    nc.vector.tensor_tensor(o4[:, :, 1, :], b4[:, :, :, 0], a4[:, :, :, 1],
                                            ALU.add).then_inc(rot_done, 1)

            def step(what, r):
                name, hd = what
                if name == "probs":
                    dve.wait_ge(score_done, n.of("SC") + 1)
                    table = decay[:, bass.ds(r * GROUP_HEADS + hd, 1), :].rearrange("p h t -> p (h t)")
                    nc.vector.tensor_tensor(probs[:, 0:S], score_ps[:, 0:S], table, ALU.mult)
                    nc.vector.tensor_tensor(probs[:, S:S + P], score_ps[:, S:S + P], table[:, 0:P],
                                            ALU.mult).then_inc(prob_done, 1)
                    n.add(SC=1)
                elif name == "norm":
                    for t in range(TT):
                        dve.wait_ge(evac, n.of("E") * TT + (t + 1))
                        nc.vector.bn_stats(y_stats[:, t, :], ybuf[:, t, :]).then_inc(bn_done, 1)
                    for t in range(TT):
                        dve.wait_ge(ret_in, 48)
                        dve.wait_ge(bn_done, n.of("Y") * TT + (t + 1))
                        nc.vector.bn_aggr(y_mv[:, t, :], y_stats[:, t, :]).then_inc(mv_done, 1)
                    dve.wait_ge(mv_done, (n.of("Y") + 1) * TT)
                    nc.vector.tensor_scalar(y_var[:], y_mv[:, :, 1], EPS, None, ALU.add).then_inc(var_done, 1)
                    for t in range(TT):
                        nc.vector.scalar_tensor_tensor(out=ybuf[:, t, :], in0=ybuf[:, t, :], scalar=y_mv[:, t, 0:1],
                                                       in1=ev[:, 0, t, :], op0=ALU.subtract,
                                                       op1=ALU.mult).then_inc(z_mul, 1)
                    n.add(E=1, Y=1)
                else:
                    for b in range(2):
                        lower_T(4 * hd + 2 * b, b)

            def retention():
                gains()
                for f in range(KT // 2):
                    split_h(f)
                dve.wait_ge(gate_in, 16 * n.of("GB"))
                dve.wait_ge(ret_in, 48)
                with dve.Fori(0, 2) as r:
                    n.enter(r, R_ROUND)
                    for i, kind in enumerate(R_KINDS):
                        hooks = {s: [lambda w=w: step(w, r) for w in ws] for s, ws in DVE_STEPS.get(i, {}).items()}
                        if i in (1, 7):
                            hooks.setdefault(4, []).append(lambda: n.add(TB=2))
                        if i in (2, 8):
                            hooks.setdefault(3, []).append(lambda: n.add(TB=2))
                        if i == R_UNITS - 1:
                            hooks[2] = [lambda: take_rows(0, 4)]
                        steps(hooks, sum(ADA_RET[:i]), ADA_RET[i])
                        if kind in ("q", "k"):
                            rotate(i % 2, i)
                        elif kind == "m2":
                            add_block(i % 2, i - 12)
                        n.unit(kind)
                    n.add(SB=3)
                    n.add(CS=1)
                    take_column(bass.ds(r + 6, 1))
                n.leave(2)

            def between():
                mean_square()
                diagonals()

            mlp(0)
            between()
            retention()
            between()
            mlp(1)
            mean_square()
            dve.wait_ge(final_in, 16)
            for t in range(TT):
                dve.wait_ge(xn_done, t + 1)
                nc.vector.tensor_tensor(x[:, t, :], x[:, t, :], final_gain, ALU.mult).then_inc(o_ready, 1)

        @block.gpsimd
        def _(pool):
            n = Count()

            def inverse_root():
                pool.wait_ge(ms_done, n.n["NO"] + 1)
                nc.gpsimd.tensor_tensor(rstd[:], meansq[:], minus_half[:], ALU.pow).then_inc(rstd_done, 1)
                n.add(NO=1)

            nc.gpsimd.memset(col_rows[:], 0.0)
            nc.gpsimd.memset(rows[:], 0.0).then_inc(rows_zero, 1)
            nc.gpsimd.memset(ones[:], 1.0).then_inc(ones_set, 1)
            nc.gpsimd.memset(minus_half[:], -0.5).then_inc(half_set, 1)
            pool.wait_ge(half_set, 1)
            for _ in range(3):
                inverse_root()
            for hd in range(HEADS):
                pool.wait_ge(var_done, hd + 1)
                nc.gpsimd.tensor_tensor(y_rstd[:], y_var[:], minus_half[:], ALU.pow).then_inc(z_rstd, 1)
            for _ in range(2):
                inverse_root()


_INS = ["x", "c", "ada_w", "ada_b", "norm_g", "pool_w", "pool_scale", "ret_w_in", "ret_w_out", "mlp_w1", "mlp_w2",
        "final_g"]


def tables():
    ident = np.eye(P, dtype=np.float32)
    inv = np.float32(10000.0) ** (-np.arange(0, 2 * P, 2, dtype=np.float32) / np.float32(2 * P))
    ang = (np.arange(S, dtype=np.float32)[:, None] * inv[None, :]).astype(np.float64)

    def by_token(a):
        return np.ascontiguousarray(np.repeat(a, 2, axis=1).reshape(TT, P, 2 * P).transpose(1, 0, 2).astype(np.float32))

    log_g = np.log(1.0 - 2.0 ** (-5.0 - np.arange(HEADS)))
    j = np.arange(P, dtype=np.float64)
    diff = j[None, :] - j[:, None]
    decay = np.zeros((P, HEADS, S))
    for h in range(HEADS):
        decay[:, h, 0:P] = np.where(diff >= 0, np.exp(np.maximum(diff, 0.0) * log_g[h]), 0.0)
        decay[:, h, P:S] = np.exp((j[None, :] + 1.0) * log_g[h]) * np.exp((P - 1.0 - j[:, None]) * log_g[h])
    decay *= (2 * P) ** -0.5
    rcount = np.broadcast_to(1.0 / np.arange(1, 17), (P, 4, 16))
    return dict(ident=ident, cos=by_token(np.cos(ang)), sin=by_token(np.sin(ang)),
                decay=decay.astype(np.float32), rcount=np.ascontiguousarray(rcount.astype(np.float32)))


def kernel(**inputs):
    import concourse.bacc as _bacc
    from concourse.bass_utils import run_bass_kernel_spmd as _run

    nc = _bacc.Bacc("TRN2", target_bir_lowering=False, num_devices=1,
                     dynamic_dma_scratch_size=8192)
    arrays, args = {}, []
    data = {name: np.ascontiguousarray(inputs[name]) for name in _INS}
    data.update(tables())
    for name, a in data.items():
        arrays[f"in_{name}"] = a
        args.append(nc.dram_tensor(f"in_{name}", a.shape, mybir.dt.from_np(a.dtype), kind="ExternalInput").ap())
    out = nc.dram_tensor("out_0", (1, S, D), F32, kind="ExternalOutput").ap()
    program(nc, *args, out)
    r = _run(nc, [arrays], core_ids=[0])
    return r.results[0]["out_0"]
```

```python
from contextlib import ExitStack

import numpy as np

import concourse.bass as bass
from concourse import mybir

ALU = mybir.AluOpType
ACT = mybir.ActivationFunctionType
AX_X = mybir.AxisListType.X
F32 = mybir.dt.float32
F32R = mybir.dt.float32r

P = 128
D = 2048
S = 256
TT = S // P
KT = D // P
NB = 512
CH = 8
CK = KT // CH
RING = 4
LEAD = RING
AW = 1024
SEG = KT * D // AW
HEADS = 8
GROUP_HEADS = 4
EPS = 1e-6
WINDOWS = (2, 4, 8, 16)
P_WIN = (1, 0, 0, 1)
M_UNITS = 8
R_UNITS = 16

UNIT = {
    "m1": dict(U=1, E=1, SQ=1),
    "m2": dict(U=1, E=1, XA=1),
    "q": dict(U=1, E=1, RO=1),
    "k": dict(U=1, E=1, RO=1),
    "g": dict(U=1, E=1),
    "v": dict(U=1, E=1),
}


class Count:

    NAMES = ("U", "E", "SQ", "XA", "RO", "TB", "TL", "SC", "Y", "AD", "AP", "SG", "RM",
             "TR", "TS", "CS", "GB", "NO", "GN", "HT", "SB")

    def __init__(self):
        self.n = {k: 0 for k in self.NAMES}
        self.reg, self.per = None, {}

    def add(self, **more):
        for k, v in more.items():
            self.n[k] += v

    def unit(self, kind):
        self.add(**UNIT[kind])

    def of(self, k):
        per = self.per.get(k, 0)
        return self.n[k] if self.reg is None or per == 0 else self.reg * per + self.n[k]

    def enter(self, reg, per):
        self.reg, self.per, self.kept = reg, per, dict(self.n)

    def leave(self, trips):
        for k in self.NAMES:
            seen = self.n[k] - self.kept[k]
            assert seen <= self.per.get(k, 0), (k, seen, self.per)
            self.n[k] = self.kept[k] + trips * self.per.get(k, 0)
        self.reg, self.per = None, {}


M_KINDS = ["m1"] * 4 + ["m2"] * 4
PAIR = ["q", "k", "g", "v", "g", "v"]
R_KINDS = PAIR * 2 + ["m2"] * 4

ADA_GATE_NOW = ([4, 6, 6, 6, 5, 5, 0, 0], "now")
ADA_COL = ([5, 5, 5, 5, 4, 4, 4, 0], "col")
ADA_GATE_KEPT = ([5, 5, 5, 5, 4, 4, 4, 0], "kept")
ADA_NONE = ([0] * 8, None)
ADA_RET = [3] * 2 + [2] * 13 + [0]
M_ROUND = dict(U=8, E=8, SQ=4, XA=4, TB=8, TL=8, SB=3)
R_ROUND = dict(U=16, E=20, XA=4, RO=4, TB=16, TL=8, SC=4, Y=4, AD=SEG, SG=1, RM=1, TR=1, TS=1, CS=1, SB=3)


def mlp_round(plan):
    spread, what = plan
    return dict(M_ROUND, AD=sum(spread), **(dict(SG=1, RM=1, TR=1, TS=1, CS=1) if what == "col" else {}))


MLP_PLAN = {
    0: [(0, 1, ADA_GATE_NOW), (1, 2, ADA_COL), (3, 1, ADA_GATE_KEPT)],
    1: [(0, 1, ADA_GATE_NOW), (1, 2, ADA_NONE), (3, 1, ADA_NONE)],
}

PE_STEPS = {1: {4: ["T rot"]}, 2: {3: ["T rot"]}, 3: {1: [("scores", 0)]}, 4: {3: [("weigh", 0)]},
            5: {1: [("scores", 1)], 3: ["T z"]},
            6: {3: [("weigh", 1)]}, 7: {2: ["T z"], 4: ["T rot"]}, 8: {3: ["T rot"]},
            9: {1: [("scores", 2)]}, 10: {3: [("weigh", 2)]}, 11: {1: [("scores", 3)], 3: ["T z"]},
            12: {0: [("weigh", 3)], 3: ["T z"]}}
ACT_STEPS = {1: {4: [("q",)]}, 2: {3: [("k",)]}, 4: {3: [("y", 0)]}, 5: {1: [("z", 0)], 3: [("a", 0)]},
             6: {3: [("y", 1)]}, 7: {0: [("z", 1)], 2: [("a", 1)], 4: [("q",)]}, 8: {3: [("k",)]},
             10: {3: [("y", 2)]}, 11: {1: [("z", 2)], 3: [("a", 2)]},
             12: {0: [("y", 3)], 1: [("z", 3)], 3: [("a", 3)]}}
DVE_STEPS = {3: {1: [("probs", 0)]}, 4: {3: [("norm", 0)]}, 5: {1: [("probs", 1)], 3: [("lo", 0)]},
             6: {3: [("norm", 1)]}, 7: {2: [("lo", 1)]},
             9: {1: [("probs", 2)]}, 10: {3: [("norm", 2)]}, 11: {1: [("probs", 3)], 3: [("lo", 2)]},
             12: {0: [("norm", 3)], 3: [("lo", 3)]}}


def program(nc, x_in, c_in, ada_w, ada_b, norm_g, pool_w, pool_scale, ret_w_in, ret_w_out, mlp_w1, mlp_w2,
            final_g, ident_in, cos_in, sin_in, decay_in, rcount_in, out):
    with ExitStack() as ctx:
        def sb(name, shape, dt=F32):
            return ctx.enter_context(nc.sbuf_tensor(name, shape, dt))

        def sem(name):
            return ctx.enter_context(nc.semaphore(name))

        raw = sb("raw", [P, RING, CK, NB])
        w_hi = sb("w_hi", [P, RING, CK, NB], F32R)
        w_lo = sb("w_lo", [P, RING, CK, NB], F32R)
        ada_raw = sb("ada_raw", [P, RING, AW])
        ada_acc = sb("ada_acc", [P, D])
        seg_row = sb("seg_row", [P, NB])
        bias_row = sb("bias_row", [P, NB])
        scale_row = sb("scale_row", [P, NB])
        col_rows = sb("col_rows", [P, P])
        x = sb("x", [P, TT, D])
        h_hi = sb("h_hi", [P, KT, S], F32R)
        h_lo = sb("h_lo", [P, KT, S], F32R)
        a_hi = sb("a_hi", [P, KT, S], F32R)
        a_lo = sb("a_lo", [P, KT, S], F32R)
        gate = sb("gate", [P, D])
        ev = sb("ev", [P, 2, TT, NB])
        ident = sb("ident", [P, P])
        ones = sb("ones", [P, P])
        diag = sb("diag", [P, TT, P])
        rows = sb("rows", [P, 2, P])
        norm_col = sb("norm_col", [P, 4, KT])
        mod_col = sb("mod_col", [P, 8, KT])
        gain_col = sb("gain_col", [P, 4, KT])
        cond = sb("cond", [P, KT])
        rcount = sb("rcount", [P, 4, 16])
        sq_junk = sb("sq_junk", [P, TT, NB], mybir.dt.bfloat16)
        ssq = sb("ssq", [P, TT, 4])
        ssum = sb("ssum", [P, TT])
        meansq = sb("meansq", [P, TT])
        rstd = sb("rstd", [P, TT])
        minus_half = sb("minus_half", [P, TT])
        y_stats = sb("y_stats", [P, TT, 6])
        y_mv = sb("y_mv", [P, TT, 2])
        y_var = sb("y_var", [P, TT])
        y_rstd = sb("y_rstd", [P, TT])
        scratch = sb("scratch", [P, 8192 + 384])
        h32 = scratch[:, 0:4096].rearrange("p (k t) -> p k t", k=KT)
        win = [scratch[:, 4096 + 1024 * i:5120 + 1024 * i].rearrange("p (k t) -> p k t", k=4) for i in range(2)]
        hbuf = [scratch[:, 512 * i:512 * (i + 1)].rearrange("p (k t) -> p k t", k=2) for i in range(2)]
        ybuf = scratch[:, 0:1024].rearrange("p (t n) -> p t n", t=TT)
        rot_a = scratch[:, 1024:1536]
        rot_b = scratch[:, 1536:2048]
        rot = scratch[:, 2048:3072].rearrange("p (t n) -> p t n", t=TT)
        qT = scratch[:, 3072:4096].rearrange("p (k t) -> p k t", k=4)
        kT = scratch[:, 4096:5120].rearrange("p (k t) -> p k t", k=4)
        decay = scratch[:, 5120:7168].rearrange("p (h t) -> p h t", h=HEADS)
        cos = scratch[:, 7168:7680].rearrange("p (t i) -> p t i", t=TT)
        sin = scratch[:, 7680:8192].rearrange("p (t i) -> p t i", t=TT)
        probs = scratch[:, 8192:8192 + 384]
        y_end = scratch[:, 0:4096].rearrange("p (t n) -> p t n", t=TT)
        final_gain = scratch[:, 4096:6144]

        acc = [[ctx.enter_context(nc.psum_tensor(f"acc{p}{t}", [P, NB], F32)) for t in range(TT)] for p in range(2)]
        tb = [ctx.enter_context(nc.psum_tensor(f"tb{i}", [P, NB], F32)) for i in range(2)]
        mod_ps = ctx.enter_context(nc.psum_tensor("mod_ps", [P, NB], F32))
        score_ps = ctx.enter_context(nc.psum_tensor("score_ps", [P, NB], F32))

        raw_in = [sem(f"raw_in{i}") for i in range(RING)]
        ada_in = [sem(f"ada_in{i}") for i in range(RING)]
        x_loaded = sem("x_loaded")
        rows_in = sem("rows_loaded")
        const_in = sem("const_loaded")
        bias_in = sem("bias_row_loaded")
        ret_in = sem("ret_tables_loaded")
        scale_in = sem("layer_scale_loaded")
        final_in = sem("final_g_loaded")
        out_done = sem("out_done")
        rows_zero = sem("rows_zero")
        ones_set = sem("ones_set")
        half_set = sem("half_set")
        cond_rows = sem("cond_rows")
        setup_T = sem("setup_transposed")
        setup_col = sem("setup_columns")
        hi_ready = sem("hi_ready")
        lo_ready = sem("lo_ready")
        w_used = sem("w_used")
        evac = sem("evac_done")
        sq_done = sem("squared")
        tr_done = sem("tr_bank_filled")
        tevac = sem("tr_bank_evacuated")
        tlo = sem("tr_bank_split")
        mul_done = sem("gated")
        x_added = sem("x_added")
        ab_done = sem("rot_products")
        rot_done = sem("rotated")
        score_done = sem("scores")
        prob_done = sem("probs")
        y_ready = sem("y_summed")
        bn_done = sem("y_stats_done")
        mv_done = sem("y_mv_done")
        var_done = sem("y_var_done")
        z_rstd = sem("y_rstd_done")
        z_mul = sem("z_gated")
        z_done = sem("z_scaled")
        ada_done = sem("ada_done")
        ada_pe = sem("ada_rows_multiplied")
        row_mm = sem("row_summed")
        row_biased = sem("row_biased")
        row_ready = sem("seg_row_ready")
        col_rows_in = sem("col_rows_in")
        col_T = sem("col_transposed")
        col_used = sem("mod_col_ready")
        gate_in = sem("gate_in")
        gain_ready = sem("gain_ready")
        ssq_done = sem("ssq_done")
        ssum_done = sem("ssum_done")
        ms_done = sem("meansq_done")
        rstd_done = sem("rstd_done")
        diag_ready = sem("diag_ready")
        hhi_done = sem("h_hi_done")
        h_ready = sem("h_ready")
        pool_step = sem("pool_step")
        p_ready = sem("p_ready")
        p_hi = sem("p_hi")
        p_lo = sem("p_lo")
        y_gained = sem("x_gained")
        xn_done = sem("out_ready_tile_1")
        o_ready = sem("out_ready_tile_0")

        block = ctx.enter_context(nc.Block())

        @block.sync
        def _(sp):
            n = Count()
            ada_flat = ada_w.rearrange("i s d (j k) -> (i s) d j k", j=3)

            def load_chunk(c, source):
                if n.reg is not None or CH * n.of("U") + c >= RING:
                    sp.wait_ge(lo_ready, n.of("U") * CH + (c - RING + 1))
                sp.dma_start(raw[:, c % RING], source).then_inc(raw_in[c % RING], 16)

            def load_ada(seg, a, shared=False):
                if shared:
                    if a % 2:
                        if n.n["AP"] >= 2:
                            sp.wait_ge(ada_pe, n.n["AP"] - 1)
                    elif n.n["AD"] >= 2:
                        sp.wait_ge(ada_done, n.n["AD"] - 1)
                elif n.reg is None and n.n["AD"] < n.n["AP"] + RING:
                    sp.wait_ge(ada_done, n.n["AP"])
                    sp.wait_ge(ada_pe, n.n["AP"])
                else:
                    sp.wait_ge(ada_done, n.of("AD") - (RING - 1))
                norm, part = (seg // 3, seg % 3) if isinstance(seg, int) else seg
                src = ada_flat[norm, (a % KT) * P:(a % KT + 1) * P, bass.ds(part, 1),
                               (a // KT) * AW:(a // KT + 1) * AW].rearrange("p j k -> p (j k)")
                sp.dma_start(ada_raw[:, a % RING], src).then_inc(ada_in[a % RING], 16)
                if shared and a % 2:
                    n.add(AP=1)
                else:
                    n.add(AD=1)

            def unit(kind, source, seg, a0, count, c0=0):
                behind = {c: [] for c in range(CH)}
                for j in range(count):
                    step = next(s for s in range(CH) if count * (s + 1) // CH > j)
                    behind[max(c0, min(CH - 1, step + 2))].append(a0 + j)
                for c in range(c0, CH):
                    load_chunk(c, source(c))
                    for a in behind[c]:
                        load_ada(seg, a)
                n.unit(kind)

            def rows_of(weights, col):
                return lambda c: weights[c * CK * P:(c + 1) * CK * P, col].rearrange("(k p) n -> p k n", p=P)

            def group_rows_of(weights, g, block_):
                grouped = weights.rearrange("(g k p) n -> g p k n", k=KT, p=P)
                return lambda c: grouped[bass.ds(g, 1), :, c * CK:(c + 1) * CK,
                                         block_ * NB:(block_ + 1) * NB].rearrange("g p k n -> p (g k) n")

            sp.wait_ge(rows_zero, 1)
            sp.dma_start(rows[0:KT, 1, :], c_in.rearrange("b (k p) -> (b k) p", p=P)).then_inc(rows_in, 16)
            sp.dma_start(rows[0:64, 0, :], norm_g.rearrange("i s (k p) -> (i s k) p", p=P)).then_inc(rows_in, 16)
            sp.dma_start(ident[:], ident_in).then_inc(const_in, 16)
            sp.dma_start(rcount[:], rcount_in).then_inc(const_in, 16)
            for a in range(RING):
                load_ada(0, a, True)
            for t in range(TT):
                sp.dma_start(x[:, t, :], x_in[0, t * P:(t + 1) * P, :]).then_inc(x_loaded, 16)
            for a in range(RING, SEG):
                load_ada(0, a, True)
            for a in range(SEG):
                load_ada(1, a, True)
            pool_rows = rows_of(pool_w.rearrange("l g c n -> (l g c) n"), slice(0, NB))
            for c in range(RING):
                load_chunk(c, pool_rows(c))
            for a in range(SEG):
                load_ada(2, a, True)
            for a in range(SEG):
                load_ada(3, a, True)
                if a % 4 == 3 and a < 16:
                    load_chunk(RING + a // 4, pool_rows(RING + a // 4))
            n.add(U=1)
            for a in range(SEG):
                load_ada(4, a, True)
                if KT < a < KT + 2 * LEAD and a % 2:
                    load_chunk((a - KT) // 2, rows_of(mlp_w1[0], slice(0, NB))((a - KT) // 2))

            def mlp(layer):
                for first, trips, plan in MLP_PLAN[layer]:
                    spread, what = plan
                    kept_seg = {(0, 0): 5, (0, 3): 8, (1, 0): 11}.get((layer, first))

                    def group(g, seg):
                        for u in range(M_UNITS):
                            if u < 4:
                                source = rows_of(mlp_w1[layer], bass.ds(g * (4 * NB) + u * NB, NB))
                            else:
                                source = group_rows_of(mlp_w2[layer], g, u - 4)
                            unit(M_KINDS[u], source, seg, sum(spread[:u]), spread[u],
                                 LEAD if (layer, first, u) == (0, 0, 0) else 0)

                    if trips == 1:
                        group(first, kept_seg)
                    else:
                        with sp.Fori(0, trips) as r:
                            n.enter(r, mlp_round(plan))
                            group(r + first, (2, r))
                        n.leave(trips)

            def retention():
                with sp.Fori(0, 2) as r:
                    n.enter(r, R_ROUND)
                    for i, kind in enumerate(R_KINDS):
                        pair, w = i // 6, i % 6
                        if kind == "m2":
                            source = group_rows_of(ret_w_out[0], r, i - 12)
                        else:
                            if kind in "qk":
                                col = r * (2 * NB) + (D * (kind == "k") + pair * NB)
                            else:
                                col = r * (GROUP_HEADS * NB) + (2 * D + 2 * D * (kind == "g") +
                                                                (2 * pair + (w - 2) // 2) * NB)
                            source = rows_of(ret_w_in[0], bass.ds(col, NB))
                        unit(kind, source, (3, r), sum(ADA_RET[:i]), ADA_RET[i])
                n.leave(2)

            mlp(0)
            retention()
            mlp(1)
            for half in range(2):
                for t, ready in ((0, o_ready), (1, xn_done)):
                    cols = slice(half * AW, (half + 1) * AW)
                    sp.wait_ge(ready, half + 1)
                    sp.dma_start(out[0, t * P:(t + 1) * P, cols], x[:, t, cols]).then_inc(out_done, 16)
            sp.wait_ge(out_done, 16 * 2 * TT)

        @block.tensor
        def _(pe):
            n = Count()

            def chunk(c, lhs_hi, lhs_lo, pair, first, last):
                for j in range(CK):
                    for t in range(TT):
                        tok = slice(t * P, (t + 1) * P)
                        for i, (l, w) in enumerate(((lhs_lo, w_hi), (lhs_hi, w_lo), (lhs_hi, w_hi))):
                            mm = nc.tensor.matmul(acc[pair][t][:], l[:, CK * c + j, tok], w[:, c % RING, j, :],
                                                  start=first and j == 0 and i == 0,
                                                  stop=last and j == CK - 1 and i == 2)
                mm.then_inc(w_used, 1)

            def unit(kind, pair, hooks, lhs, ready, c0=0, c1=CH):
                for c in range(c0, c1):
                    pe.wait_ge(lo_ready, n.of("U") * CH + (c + 1))
                    ready(c)
                    if c == 0:
                        pe.wait_ge(evac, (n.of("E") - 1) * TT)
                    chunk(c, *lhs, pair, c == 0, c == CH - 1)
                    for hook in hooks.get(c, []):
                        hook()
                if c1 == CH:
                    n.unit(kind)

            def ready_h(c):
                pe.wait_ge(h_ready, n.n["HT"] - CH + c + 1)

            def transposes(source, split):
                for b in range(2):
                    pe.wait_ge(tevac, n.of("TB") + (b - 1))
                    pe.wait_ge(tlo, n.of("TL"))
                    for j in range(2):
                        for t in range(TT):
                            m = 2 * b + j
                            tr = nc.tensor.transpose(tb[b][:, j * S + t * P:j * S + (t + 1) * P],
                                                     source(t)[:, m * P:(m + 1) * P], ident[:])
                    tr.then_inc(tr_done, 1)
                n.add(TB=2, TL=2 if split else 0)

            def row_blocks(bank, b0, b1, start):
                for b in range(b0, b1):
                    mm = nc.tensor.matmul(bank[32 * b:32 * b + 32, :], ones[:, 0:32],
                                          ada_acc[:, b * NB:(b + 1) * NB], start=start, stop=True)
                mm.then_inc(row_mm, 1)
                n.add(RM=1)

            def shared_rows(seg, a0, a1):
                bank = (mod_ps, score_ps)[seg % 2]
                for a in range(a0 + 1, a1, 2):
                    k, half = a % KT, a // KT
                    if a == 1 and seg == 4:
                        pe.wait_ge(row_ready, 3)
                    elif a == 1 and seg >= 2:
                        pe.wait_ge(col_used, seg - 1)
                    pe.wait_ge(ada_in[a % RING], (seg * (SEG // RING) + a // RING + 1) * 16)
                    for b in (2 * half, 2 * half + 1):
                        mm = nc.tensor.matmul(bank[32 * b:32 * b + 32, :], cond[:, k:k + 1].to_broadcast([P, 32]),
                                              ada_raw[:, a % RING, b % 2 * NB:(b % 2 + 1) * NB], start=k == 1,
                                              stop=False)
                    mm.then_inc(ada_pe, 1)
                    n.add(AP=1)
                    if k == KT - 1:
                        n.add(AD=CH)
                        pe.wait_ge(ada_done, n.n["AD"])
                        row_blocks(bank, 2 * half, 2 * half + 2, False)

            def row_sum(b0, b1, chunks):
                pe.wait_ge(ada_done, chunks)
                pe.wait_ge(row_ready, n.of("TR"))
                pe.wait_ge(col_used, n.of("CS"))
                row_blocks(mod_ps, b0, b1, True)
                n.add(TR=1)

            def column(bank):
                pe.wait_ge(col_rows_in, 16 * (n.of("CS") + 1))
                nc.tensor.transpose(bank[:, 0:P], col_rows[:], ident[:]).then_inc(col_T, 1)
                n.add(CS=1)

            def norm_fill(f):
                if n.of("TB") >= 2:
                    pe.wait_ge(tevac, n.of("TB") - 1)
                if f < 2 and n.of("TL"):
                    pe.wait_ge(tlo, n.of("TL"))
                for j in range(2):
                    for t in range(TT):
                        k = 2 * f + j
                        tr = nc.tensor.matmul(tb[f % 2][:, j * S + t * P:j * S + (t + 1) * P],
                                              x[:, t, k * P:(k + 1) * P], diag[:, t, :], start=True, stop=True)
                tr.then_inc(tr_done, 1)
                n.add(TB=1)

            def norm(banks=KT // 2):
                pe.wait_ge(diag_ready, n.of("NO") + 1)
                for f in range(banks):
                    norm_fill(f)
                n.add(NO=1)

            pe.wait_ge(const_in, 32)
            pe.wait_ge(cond_rows, 1)
            for i in range(2):
                tr = nc.tensor.transpose(tb[0][:, i * P:(i + 1) * P], rows[:, i, :], ident[:])
            tr.then_inc(setup_T, 1)
            pe.wait_ge(ones_set, 1)
            pe.wait_ge(setup_col, 1)
            shared_rows(0, 0, SEG)
            shared_rows(1, 0, 16)
            column(mod_ps)
            shared_rows(1, 16, SEG)
            shared_rows(2, 0, 8)
            column(score_ps)
            norm(2)
            for f in range(2, KT // 2):
                shared_rows(2, 4 + 2 * f, 6 + 2 * f)
                norm_fill(f)
            shared_rows(2, 20, SEG)
            ada_at = (0, 4, 8, 12, 24, 26, 28, 30, SEG)
            for gi in range(4):
                for c in (2 * gi, 2 * gi + 1):
                    shared_rows(3, ada_at[c], ada_at[c + 1])
                    pe.wait_ge(lo_ready, c + 1)
                    if c == 2 * gi:
                        pe.wait_ge(p_lo, gi + 1)
                        if gi >= 2:
                            pe.wait_ge(evac, (gi - 1) * TT)
                    chunk(c, a_hi, a_lo, gi % 2, c == 2 * gi, c == 2 * gi + 1)
            n.add(U=1, E=4)
            shared_rows(4, 0, 12)
            column(score_ps)
            shared_rows(4, 12, 16)
            norm(2)
            shared_rows(4, 16, 20)
            column(score_ps)
            n.add(HT=CH)
            for c in range(LEAD):
                shared_rows(4, 20 + 2 * c, 22 + 2 * c)
                if c < 2:
                    norm_fill(2 + c)
                unit("m1", 0, {}, (h_hi, h_lo), ready_h, c, c + 1)
            shared_rows(4, 28, SEG)
            norm_fill(4)
            norm_fill(5)
            column(score_ps)
            norm_fill(6)
            n.add(TR=6)

            def mlp(layer):
                if layer:
                    norm(2)
                    n.add(HT=CH)
                for first, trips, plan in MLP_PLAN[layer]:
                    spread, what = plan

                    def group():
                        split0, ada0 = n.of("TL"), n.of("AD")
                        for u in range(M_UNITS):
                            hooks = {}
                            if first == 0 and u == 0:
                                hooks = ({f - 2: [lambda f=f: norm_fill(f)] for f in range(2, KT // 2)} if layer else
                                         {LEAD: [lambda: norm_fill(KT // 2 - 1)]})
                            if what == "now" and u in (4, 6):
                                b = u - 4
                                hooks[0] = [lambda b=b: row_sum(b, b + 2, ada0 + SEG // 4 * (b + 2))]
                            elif what and what != "now" and u == 7:
                                hooks[0] = [lambda: row_sum(0, 4, n.of("AD"))]
                            if 1 <= u <= 4:
                                def transpose_squares(pair=(u - 1) % 2):
                                    pe.wait_ge(sq_done, n.of("SQ") * TT)
                                    transposes(lambda t: ev[:, pair, t, :], True)
                                hooks[2] = [transpose_squares]
                            if u < 4:
                                unit("m1", u % 2, hooks, (h_hi, h_lo), ready_h,
                                     LEAD if (layer, first, u) == (0, 0, 0) else 0)
                            else:
                                unit("m2", u % 2, hooks, (a_hi, a_lo), lambda c: pe.wait_ge(tlo, split0 + (c + 1)))
                            n.add(AD=spread[u])
                        if what == "col":
                            column(mod_ps)

                    if trips == 1:
                        group()
                    else:
                        with pe.Fori(0, trips) as r:
                            n.enter(r, mlp_round(plan))
                            group()
                        n.leave(trips)

            def scores(hd):
                pe.wait_ge(tevac, n.of("TB"))
                if hd:
                    pe.wait_ge(prob_done, n.of("SC"))
                w = (hd % 2) * 2
                for part, q0 in ((0, 0), (1, P)):
                    for j in range(2):
                        mm = nc.tensor.matmul(score_ps[:, part * S:part * S + S - q0],
                                              kT[:, w + j, part * P:(part + 1) * P], qT[:, w + j, q0:S],
                                              start=j == 0, stop=j == 1)
                mm.then_inc(score_done, 1)
                n.add(SC=1)

            def weigh(pair):
                pe.wait_ge(prob_done, n.of("Y") + 1)
                pe.wait_ge(evac, n.of("E") * TT)
                nc.tensor.matmul(acc[pair][0][:], probs[:, 0:P], ev[:, 1, 0, :], start=True, stop=True)
                nc.tensor.matmul(acc[pair][1][:], probs[:, P:S], ev[:, 1, 0, :], start=True, stop=False)
                nc.tensor.matmul(acc[pair][1][:], probs[:, S:S + P], ev[:, 1, 1, :], start=False,
                                 stop=True).then_inc(y_ready, 1)
                n.add(E=1, Y=1)

            def transpose_rotated():
                pe.wait_ge(rot_done, n.of("RO") * TT)
                transposes(lambda t: rot[:, t, :], False)

            def transpose_z():
                pe.wait_ge(z_done, n.of("Y"))
                transposes(lambda t: ybuf[:, t, :], True)

            def retention():
                norm()
                n.add(HT=CH)
                with pe.Fori(0, 2) as r:
                    n.enter(r, R_ROUND)
                    split0 = n.of("TL")
                    for i, kind in enumerate(R_KINDS):
                        hooks = {}
                        for c, steps in PE_STEPS.get(i, {}).items():
                            hooks[c] = [transpose_rotated if s == "T rot" else transpose_z if s == "T z" else
                                        (lambda s=s, i=i: scores(s[1]) if s[0] == "scores" else weigh((i - 1) % 2))
                                        for s in steps]
                        if i == R_UNITS - 1:
                            hooks[0] = [lambda: row_sum(0, 4, n.of("AD"))]
                        if kind == "m2":
                            unit(kind, i % 2, hooks, (a_hi, a_lo), lambda c: pe.wait_ge(tlo, split0 + (c + 1)))
                        else:
                            unit(kind, i % 2, hooks, (h_hi, h_lo), ready_h)
                        n.add(AD=ADA_RET[i])
                    column(mod_ps)
                n.leave(2)

            mlp(0)
            retention()
            mlp(1)

        @block.scalar
        def _(act):
            n = Count()

            def hi(c, ahead=0):
                u = n.of("U") + ahead
                act.wait_ge(raw_in[c % RING], (u * 2 + (c // RING + 1)) * 16)
                if not (n.reg is None and u * CH + c < RING):
                    act.wait_ge(w_used, u * CH + (c - RING + 1))
                nc.scalar.activation(w_hi[:, c % RING], raw[:, c % RING], ACT.Copy).then_inc(hi_ready, 1)

            def steps(hooks, ahead=LEAD, taken=0):
                for s in range(CH):
                    if s < taken:
                        pass
                    elif s < CH - LEAD:
                        hi(s + LEAD)
                    elif s < CH - LEAD + ahead:
                        hi(s + LEAD - CH, 1)
                    for hook in hooks.get(s, []):
                        hook()

            def evacuate(pair, func, target):
                for t in range(TT):
                    nc.scalar.activation(target[:, t, :], acc[pair][t][:], func).then_inc(evac, 1)
                n.add(E=1)

            def evacuate_T(targets, b):
                act.wait_ge(tr_done, n.of("TB") + 1)
                nc.scalar.activation(targets, tb[b][:].rearrange("p (k t) -> p k t", k=2), ACT.Copy).then_inc(tevac, 1)
                n.add(TB=1)

            def squares(block_, fresh=False):
                for t in range(TT):
                    if fresh:
                        act.wait_ge(x_added, (n.of("XA") - 1) * TT + t + 1)
                    if n.reg is not None or n.of("SB"):
                        act.wait_ge(ssq_done, (n.of("SB") - 1) * TT + t + 1)
                    nc.scalar.activation(sq_junk[:, t, :], x[:, t, block_ * NB:(block_ + 1) * NB], ACT.Square,
                                         accum_out=ssq[:, t, block_:block_ + 1]).then_inc(ssq_done, 1)
                n.add(SB=1)

            def unit_done():
                act.wait_ge(w_used, (n.of("U") + 1) * CH)

            def norm_evac(f, target):
                act.wait_ge(tr_done, n.of("TB") + 1)
                k0 = n.n["NO"]
                for j in range(2):
                    k = 2 * f + j
                    h = nc.scalar.activation(target[:, j, :], tb[f % 2][:, j * S:(j + 1) * S], ACT.Identity,
                                             bias=mod_col[:, 2 * k0, k:k + 1], scale=gain_col[:, k0, k:k + 1])
                h.then_inc(tevac, 1)
                n.add(TB=1)
                if f == KT // 2 - 1:
                    n.add(NO=1)

            def norm_bank(f):
                if f == 0 or f == KT // 4 and n.n["NO"] == 1:
                    act.wait_ge(gain_ready, n.n["GN"] + 1)
                    n.add(GN=1)
                if f >= 2:
                    act.wait_ge(h_ready, n.n["HT"] + f - 1)
                norm_evac(f, hbuf[f % 2])
                if f == KT // 2 - 1:
                    n.add(HT=CH)

            def by_block(row):
                return row.rearrange("(b o n) -> b o n", b=4, o=1).to_broadcast([4, 32, NB])

            def load_bias(norm_, part):
                row = ada_b.rearrange("i s (j k) -> (i s) j k", j=3)[norm_, bass.ds(part, 1), :]
                act.dma_start(bias_row[:], by_block(row.rearrange("j k -> (j k)"))).then_inc(bias_in, 16)

            def send_column(b0=0, b1=4):
                act.wait_ge(row_ready, n.of("TR") + 1)
                if n.n["CS"]:
                    act.wait_ge(col_T, n.of("CS"))
                else:
                    act.wait_ge(rows_zero, 1)
                act.dma_start(col_rows[4 * b0:4 * b1, :],
                              seg_row[32 * b0:32 * b1:32, :].rearrange("p (m c) -> p m c", m=4)).then_inc(col_rows_in, 16)
                n.add(TR=1, CS=1)

            def send_gate(b0, b1):
                act.wait_ge(row_ready, n.of("TR") + 1)
                if n.n["XA"]:
                    act.wait_ge(x_added, n.n["XA"] * TT)
                for b in range(b0, b1):
                    row = seg_row[32 * b:32 * b + 1, :].rearrange("p (o n) -> p o n", o=1).to_broadcast([1, P, NB])
                    act.dma_start(gate[:, b * NB:(b + 1) * NB], row).then_inc(gate_in, 16)
                n.add(TR=1)

            load_bias(0, 0)
            act.dma_start(scale_row[:], by_block(pool_scale.rearrange("a k -> (a k)"))).then_inc(scale_in, 16)
            act.wait_ge(rows_in, 16 * 2)
            nc.scalar.activation(rows[:, 1, :], rows[:, 1, :], ACT.Silu).then_inc(cond_rows, 1)
            act.wait_ge(x_loaded, 16 * TT)
            for b in range(4):
                squares(b)
            for seg in range(2):
                send_column()
                load_bias(0, seg + 1)
            act.wait_ge(gain_ready, 1)
            n.add(GN=1)
            for f in range(4):
                norm_evac(f, h32[:, 2 * f:2 * f + 2, :])
            def evacuate_group(gi):
                act.wait_ge(w_used, 2 * gi + 2)
                if gi >= 2:
                    act.wait_ge(x_added, (gi - 1) * TT)
                evacuate(gi % 2, ACT.Copy, ev[:, gi % 2])

            for gi in range(4):
                act.wait_ge(p_ready, gi + 1)
                nc.scalar.activation(a_hi[:, 4 * gi:4 * gi + 4, :], win[P_WIN[gi]], ACT.Copy).then_inc(p_hi, 1)
                if gi < 2:
                    for f in (4 + 2 * gi, 5 + 2 * gi):
                        norm_evac(f, h32[:, 2 * f:2 * f + 2, :])
                if gi < 3:
                    hi(2 * gi)
                    hi(2 * gi + 1)
                if gi == 2:
                    evacuate_group(0)
            hi(CH - 2)
            hi(CH - 1)
            evacuate_group(1)
            send_gate(0, 4)
            load_bias(1, 0)
            evacuate_group(2)
            act.wait_ge(x_added, TT)
            squares(0)
            evacuate_group(3)
            for b in range(1, 4):
                act.wait_ge(x_added, (b + 1) * TT)
                squares(b)
            n.add(XA=4)
            send_column()
            load_bias(1, 1)
            send_column(0, 2)
            hi(0, 1)
            hi(1, 1)
            norm_bank(0)
            hi(2, 1)
            norm_bank(1)
            hi(3, 1)
            norm_bank(2)
            norm_bank(3)
            n.add(U=1)
            send_column(2, 4)
            load_bias(1, 2)
            hi(LEAD)
            hi(LEAD + 1)

            def mlp(layer):
                for f in range(3) if layer else (4, 5):
                    norm_bank(f)
                for first, trips, plan in MLP_PLAN[layer]:
                    what = plan[1]

                    def group(end, r=None):
                        for u in range(M_UNITS):
                            hooks = {}
                            if first == 0 and u == 0:
                                hooks = ({f - 3: [lambda f=f: norm_bank(f)] for f in range(3, KT // 2)} if layer else
                                         {f - 6: [lambda f=f: norm_bank(f)] for f in (6, 7)})
                            if 1 <= u <= 4:
                                def upper(u=u):
                                    for b in range(2):
                                        k = 4 * (u - 1) + 2 * b
                                        evacuate_T(a_hi[:, k:k + 2, :], b)
                                hooks[2] = [upper]
                            if u > 4:
                                def block_squares(u=u):
                                    act.wait_ge(x_added, n.of("XA") * TT)
                                    squares(u - 5)
                                hooks[2] = [block_squares]
                            if what == "now" and u in (4, 6):
                                hooks.setdefault(4, []).append(lambda b=u - 4: send_gate(b, b + 2))
                                if u == 6 and layer == 0:
                                    hooks[4].append(lambda: load_bias(2, 0))
                            elif what == "col" and u == 7:
                                hooks[4] = [send_column, lambda: load_bias(2, r + 1)]
                            last = first == 3 and u == M_UNITS - 1
                            steps(hooks, LEAD if not last else 0 if end else LEAD - 1,
                                  2 if (layer, first, u) == (0, 0, 0) else 0)
                            unit_done()
                            if u < 4:
                                if u < 2:
                                    act.wait_ge(x_added, (n.of("XA") - (1 - u)) * TT)
                                evacuate(u % 2, ACT.Relu, ev[:, u % 2])
                                for t in range(TT):
                                    act.wait_ge(evac, (n.of("E") - 1) * TT + t + 1)
                                    nc.scalar.activation(ev[:, u % 2, t, :], ev[:, u % 2, t, :],
                                                         ACT.Square).then_inc(sq_done, 1)
                            else:
                                if u >= 6:
                                    act.wait_ge(x_added, (n.of("XA") - 1) * TT)
                                evacuate(u % 2, ACT.Copy, ev[:, u % 2])
                            if last and not end:
                                hi(LEAD - 1, 1)
                            n.unit(M_KINDS[u])
                            n.add(E=-1)

                    if trips == 1:
                        group(layer == 1 and first == 3)
                    else:
                        with act.Fori(0, trips) as r:
                            n.enter(r, mlp_round(plan))
                            group(False, r)
                        n.leave(trips)

            def between():
                squares(3, fresh=True)

            def retention():
                act.dma_start(decay, decay_in).then_inc(ret_in, 16)
                act.dma_start(cos, cos_in).then_inc(ret_in, 16)
                act.dma_start(sin, sin_in).then_inc(ret_in, 16)
                for f in range(KT // 2):
                    norm_bank(f)
                with act.Fori(0, 2) as r:
                    n.enter(r, R_ROUND)
                    for i, kind in enumerate(R_KINDS):
                        hooks = {s: [lambda what=w, i=i: step(what, i) for w in ws]
                                 for s, ws in ACT_STEPS.get(i, {}).items()}
                        if i > 12:
                            def block_squares(i=i):
                                act.wait_ge(x_added, n.of("XA") * TT)
                                squares(i - 13)
                            hooks[2] = [block_squares]
                        if i == R_UNITS - 1:
                            hooks[4] = [send_column, lambda: load_bias(3, r + 1)]
                        steps(hooks, LEAD - (i == R_UNITS - 1))
                        unit_done()
                        if i < 2:
                            act.wait_ge(x_added, (n.of("XA") - (1 - i)) * TT)
                        elif i in (2, 8):
                            act.wait_ge(rot_done, (n.of("RO") - 1) * TT)
                        elif i in (3, 9):
                            act.wait_ge(rot_done, n.of("RO") * TT)
                        elif i in (4, 6, 10, 12):
                            act.wait_ge(z_mul, n.of("Y") * TT)
                        elif i >= 14:
                            act.wait_ge(x_added, (n.of("XA") - 1) * TT)
                        evacuate(i % 2, ACT.Silu if kind == "g" else ACT.Copy, ev[:, i % 2])
                        if i == R_UNITS - 1:
                            hi(LEAD - 1, 1)
                        n.unit(kind)
                        n.add(E=-1)
                n.leave(2)

            def step(what, i):
                if what[0] in ("q", "k"):
                    target = qT if what[0] == "q" else kT
                    for b in range(2):
                        evacuate_T(target[:, 2 * b:2 * b + 2, :], b)
                elif what[0] == "a":
                    for b in range(2):
                        k = 4 * what[1] + 2 * b
                        evacuate_T(a_hi[:, k:k + 2, :], b)
                elif what[0] == "y":
                    act.wait_ge(y_ready, n.of("Y") + 1)
                    evacuate((i - 1) % 2, ACT.Copy, ybuf)
                    n.add(Y=1)
                else:
                    act.wait_ge(z_mul, n.of("Y") * TT)
                    act.wait_ge(z_rstd, n.of("Y"))
                    for t in range(TT):
                        z = nc.scalar.activation(ybuf[:, t, :], ybuf[:, t, :], ACT.Copy, scale=y_rstd[:, t:t + 1])
                    z.then_inc(z_done, 1)

            mlp(0)
            between()
            send_gate(0, 4)
            load_bias(3, 0)
            retention()
            between()
            act.dma_start(final_gain, final_g.rearrange("(a n) -> a n", a=1).to_broadcast([P, D])).then_inc(final_in, 16)
            mlp(1)
            between()
            act.wait_ge(rstd_done, 5)
            for half in range(2):
                cols = slice(half * AW, (half + 1) * AW)
                nc.scalar.activation(x[:, 1, cols], y_end[:, 1, cols], ACT.Copy, scale=rstd[:, 1:2]).then_inc(xn_done, 1)

        @block.vector
        def _(dve):
            n = Count()

            def lo(c, ahead=0):
                dve.wait_ge(hi_ready, (n.of("U") + ahead) * CH + (c + 1))
                nc.vector.tensor_tensor(w_lo[:, c % RING], raw[:, c % RING], w_hi[:, c % RING].bitcast(F32),
                                        ALU.subtract).then_inc(lo_ready, 1)

            def ada(a, shared=False):
                k, half = a % KT, a // KT
                if k:
                    dve.wait_ge(ada_done, n.of("AD"))
                elif shared and n.n["SG"]:
                    dve.wait_ge(row_mm, 2 * n.n["SG"] + half - 1)
                dve.wait_ge(ada_in[a % RING], (ada_round() + (a // RING + 1)) * 16)
                part = ada_acc[:, half * AW:(half + 1) * AW]
                if k:
                    nc.vector.scalar_tensor_tensor(out=part, in0=ada_raw[:, a % RING], scalar=cond[:, k:k + 1],
                                                   in1=part, op0=ALU.mult, op1=ALU.add).then_inc(ada_done, 1)
                else:
                    nc.vector.tensor_scalar(part, ada_raw[:, a % RING], cond[:, k:k + 1], None,
                                            ALU.mult).then_inc(ada_done, 1)
                n.add(AD=1)
                if a == SEG - (2 if shared else 1):
                    n.add(SG=1)

            def ada_even(a0, a1):
                for a in range(a0, a1, 2):
                    ada(a, True)

            def ada_round():
                return n.of("SG") * (SEG // RING)

            def steps(hooks, a0, count, ahead=LEAD, taken=0):
                done = 0
                for s in range(CH):
                    if s < taken:
                        pass
                    elif s < CH - LEAD:
                        lo(s + LEAD)
                    elif s < CH - LEAD + ahead:
                        lo(s + LEAD - CH, 1)
                    while done < count * (s + 1) // CH:
                        ada(a0 + done)
                        done += 1
                    for hook in hooks.get(s, []):
                        hook()

            def final_gains(b):
                blk = slice(b * NB, (b + 1) * NB)
                dve.wait_ge(final_in, 16)
                for t in range(TT):
                    dve.wait_ge(x_added, n.of("XA") * TT + (t + 1))
                    nc.vector.tensor_tensor(y_end[:, t, blk], x[:, t, blk], final_gain[:, blk], ALU.mult).then_inc(y_gained, 1)

            def take_rows(b0, b1, layer_scale=False):
                part = slice(32 * b0, 32 * b1)
                dve.wait_ge(row_mm, n.of("RM") + 1)
                dve.wait_ge(bias_in, 16 * (n.of("TS") + 1))
                if n.n["CS"]:
                    dve.wait_ge(col_rows_in, 16 * n.of("CS"))
                if n.n["GB"]:
                    dve.wait_ge(gate_in, 16 * n.of("GB"))
                row = nc.vector.tensor_tensor(seg_row[part, :], (score_ps if n.n["TS"] in (1, 3) else mod_ps)[part, :],
                                              bias_row[part, :], ALU.add)
                if layer_scale:
                    row.then_inc(row_biased, 1)
                    dve.wait_ge(scale_in, 16)
                    dve.wait_ge(row_biased, 1)
                    row = nc.vector.tensor_tensor(seg_row[:], seg_row[:], scale_row[:], ALU.mult)
                row.then_inc(row_ready, 1)
                n.add(RM=1, TR=1)
                if b1 == 4:
                    n.add(TS=1)

            def take_column(index, bank=mod_ps, k=slice(0, KT)):
                dve.wait_ge(col_T, n.of("CS"))
                nc.vector.tensor_copy(mod_col[:, index, k].rearrange("p s k -> p (s k)"),
                                      bank[:, k]).then_inc(col_used, 1)

            def add_block(p, b):
                blk = slice(b * NB, (b + 1) * NB)
                for t in range(TT):
                    dve.wait_ge(evac, n.of("E") * TT + (t + 1))
                    nc.vector.tensor_tensor(ev[:, p, t, :], ev[:, p, t, :], gate[:, blk],
                                            ALU.mult).then_inc(mul_done, 1)
                for t in range(TT):
                    dve.wait_ge(mul_done, n.of("XA") * TT + (t + 1))
                    nc.vector.tensor_tensor(x[:, t, blk], x[:, t, blk], ev[:, p, t, :], ALU.add).then_inc(x_added, 1)

            def lower_T(k, b):
                dve.wait_ge(tevac, n.of("TB") + 1)
                nc.vector.tensor_tensor(a_lo[:, k:k + 2, :], tb[b][:].rearrange("p (k t) -> p k t", k=2),
                                        a_hi[:, k:k + 2, :].bitcast(F32), ALU.subtract).then_inc(tlo, 1)
                n.add(TB=1)

            def mean_square():
                m = n.n["NO"]
                n.add(SB=4 if m < 2 else 1)
                dve.wait_ge(ssq_done, n.n["SB"] * TT)
                nc.vector.tensor_reduce(ssum[:], ssq[:], AX_X, ALU.add).then_inc(ssum_done, 1)
                dve.wait_ge(ssum_done, m + 1)
                nc.vector.tensor_scalar(meansq[:], ssum[:], 1.0 / D, EPS, ALU.mult, ALU.add).then_inc(ms_done, 1)

            def diagonals():
                m = n.n["NO"]
                dve.wait_ge(rstd_done, m + 1)
                for t in range(TT):
                    d = nc.vector.tensor_scalar(diag[:, t, :], ident[:], rstd[:, t:t + 1], None, ALU.mult)
                d.then_inc(diag_ready, 1)

            def gains(k=slice(0, KT)):
                m = n.n["NO"]
                dve.wait_ge(col_used, n.n["CS"])
                nc.vector.scalar_tensor_tensor(out=gain_col[:, m, k], in0=mod_col[:, 2 * m + 1, k], scalar=1.0,
                                               in1=norm_col[:, m, k], op0=ALU.add,
                                               op1=ALU.mult).then_inc(gain_ready, 1)
                if k.stop == KT:
                    n.add(NO=1)

            def split_h(f):
                own = n.n["HT"] + f + 1
                dve.wait_ge(tevac, n.of("TB") + 1)
                n.add(TB=1)
                nc.vector.tensor_copy(h_hi[:, 2 * f:2 * f + 2, :], hbuf[f % 2]).then_inc(hhi_done, 1)
                dve.wait_ge(hhi_done, own)
                nc.vector.tensor_tensor(h_lo[:, 2 * f:2 * f + 2, :], hbuf[f % 2],
                                        h_hi[:, 2 * f:2 * f + 2, :].bitcast(F32), ALU.subtract).then_inc(h_ready, 1)
                if f == KT // 2 - 1:
                    n.add(HT=CH)

            dve.wait_ge(setup_T, 1)
            nc.vector.tensor_copy(norm_col[:].rearrange("p s k -> p (s k)"), tb[0][:, 0:4 * KT])
            nc.vector.tensor_copy(cond[:], tb[0][:, P:P + KT]).then_inc(setup_col, 1)
            dve.wait_ge(setup_col, 1)

            def take_shared(layer_scale=False):
                n.add(RM=1)
                take_rows(0, 4, layer_scale)

            ada_even(0, 16)
            mean_square()
            ada_even(16, 24)
            diagonals()
            ada_even(24, SEG)
            ada_even(0, 8)
            take_shared()
            n.add(CS=1)
            ada_even(8, 16)
            take_column(slice(0, 1), mod_ps)
            ada_even(16, SEG)
            ada_even(0, 4)
            take_shared()
            n.add(CS=1)
            ada_even(4, 8)
            take_column(slice(1, 2), score_ps)
            gains()
            ada_even(8, 12)
            n.add(TB=CH)

            pool_count = [0]
            even_chunks = iter(list(range(12, SEG, 2)) + list(range(0, 24, 2)))

            def pool_op(ins, behind=1):
                ins.then_inc(pool_step, 1)
                pool_count[0] += 1
                for _ in range(behind):
                    ada(next(even_chunks), True)

            def own():
                dve.wait_ge(pool_step, pool_count[0])

            def pooled_lo(gi):
                dve.wait_ge(p_hi, gi + 1)
                nc.vector.tensor_tensor(a_lo[:, 4 * gi:4 * gi + 4, :], win[P_WIN[gi]],
                                        a_hi[:, 4 * gi:4 * gi + 4, :].bitcast(F32), ALU.subtract).then_inc(p_lo, 1)

            for gi, w in enumerate(WINDOWS):
                dve.wait_ge(tevac, 2 * gi + 2)
                h = h32[:, 4 * gi:4 * gi + 4, :]
                at = 1 - P_WIN[gi - 1] if gi else 0
                cur, s = h, 1
                while s < w:
                    dst = win[at]
                    if s > 1:
                        own()
                    pool_op(nc.vector.tensor_tensor(dst[:, :, s:], cur[:, :, s:], cur[:, :, :S - s], ALU.add), 1)
                    pool_op(nc.vector.tensor_copy(dst[:, :, :s], cur[:, :, :s]), 0)
                    cur, at = dst, 1 - at
                    if gi and s == 1:
                        pooled_lo(gi - 1)
                        dve.wait_ge(p_lo, gi)
                    s = 2 * s
                p = win[at]
                assert at == P_WIN[gi]
                own()
                pool_op(nc.vector.scalar_tensor_tensor(out=p, in0=cur, scalar=1.0 / w, in1=h, op0=ALU.mult,
                                                       op1=ALU.subtract))
                own()
                pool_op(nc.vector.tensor_tensor(p[:, :, :w], cur[:, :, :w], rcount[:, :, :w], ALU.mult), 1)
                own()
                nc.vector.tensor_tensor(p[:, :, :w], p[:, :, :w], h[:, :, :w], ALU.subtract).then_inc(p_ready, 1)
                ada(next(even_chunks), True)
                if gi:
                    lo(2 * gi - 2)
                    lo(2 * gi - 1)
            pooled_lo(3)
            for a in even_chunks:
                ada(a, True)
            take_shared(True)
            n.add(GB=4)
            ada_even(24, 26)
            for c in (CH - 2, CH - 1):
                lo(c)
                ada_even(14 + 2 * c, 16 + 2 * c)
            ada_even(30, SEG)
            dve.wait_ge(gate_in, 16 * 4)
            for gi in range(4):
                add_block(gi % 2, gi)
                n.add(E=1, XA=1)
                a = 2 * gi
                ada_even(a, a + 2)
            take_shared()
            n.add(CS=1)
            ada_even(8, 12)
            mean_square()
            diagonals()
            take_column(slice(2, 3), score_ps)
            ada_even(12, 18)
            take_rows(0, 2)
            n.add(CS=1)
            ada_even(18, 20)
            lo(0, 1)
            ada_even(20, 22)
            lo(1, 1)
            take_column(slice(3, 4), score_ps, slice(0, KT // 2))
            gains(slice(0, KT // 2))
            ada_even(22, 24)
            split_h(0)
            split_h(1)
            ada_even(24, 26)
            lo(2, 1)
            ada_even(26, 28)
            lo(3, 1)
            split_h(2)
            ada_even(28, 30)
            split_h(3)
            ada_even(30, SEG)
            n.add(U=1)
            take_rows(2, 4)
            n.add(CS=1)
            lo(LEAD)
            take_column(slice(3, 4), score_ps, slice(KT // 2, KT))
            gains(slice(KT // 2, KT))
            lo(LEAD + 1)
            split_h(4)

            def mlp(layer):
                if layer:
                    gains()
                    for f in range(3):
                        split_h(f)
                for first, trips, plan in MLP_PLAN[layer]:
                    spread, what = plan

                    def group(r, end):
                        for u in range(M_UNITS):
                            hooks = {}
                            if first == 0 and u == 0:
                                hooks = ({f - 3: [lambda f=f: split_h(f)] for f in range(3, KT // 2)} if layer else
                                         {f - 5: [lambda f=f: split_h(f)] for f in (5, 6, 7)})
                            if 1 <= u <= 4:
                                def lower(u=u):
                                    for b in range(2):
                                        lower_T(4 * (u - 1) + 2 * b, b)
                                hooks[2] = [lower]
                            if what == "now" and u in (4, 6):
                                def take_gate(b=u - 4):
                                    take_rows(b, b + 2)
                                    n.add(GB=2)
                                hooks.setdefault(2, []).append(take_gate)
                            elif what and what != "now" and u == 7:
                                hooks[2] = [lambda: take_rows(0, 4)]
                            last = first == 3 and u == M_UNITS - 1
                            steps(hooks, sum(spread[:u]), spread[u], LEAD if not last else 0 if end else LEAD - 1,
                                  2 if (layer, first, u) == (0, 0, 0) else 0)
                            if u >= 4:
                                if what == "now":
                                    dve.wait_ge(gate_in, 16 * n.of("GB"))
                                add_block(u % 2, u - 4)
                                if end:
                                    final_gains(u - 4)
                            if last and not end:
                                lo(LEAD - 1, 1)
                            n.unit(M_KINDS[u])
                        n.add(SB=3)
                        if what == "col":
                            n.add(CS=1)
                            take_column(bass.ds(r + 4, 1))
                        elif what == "kept":
                            n.add(GB=4)

                    if trips == 1:
                        group(0, layer == 1 and first == 3)
                    else:
                        with dve.Fori(0, trips) as r:
                            n.enter(r, mlp_round(plan))
                            group(r, False)
                        n.leave(trips)

            def rotate(p, i):
                for t in range(TT):
                    src = ev[:, p, t, :].rearrange("p (h i) -> p h i", h=2)
                    dve.wait_ge(evac, n.of("E") * TT + (t + 1))
                    a3 = rot_a.rearrange("p (h i) -> p h i", h=2)
                    b3 = rot_b.rearrange("p (h i) -> p h i", h=2)
                    if t:
                        dve.wait_ge(rot_done, n.of("RO") * TT + t)
                    nc.vector.tensor_tensor(a3, src, cos[:, t:t + 1, :].to_broadcast([P, 2, 2 * P]), ALU.mult)
                    nc.vector.tensor_tensor(b3, src, sin[:, t:t + 1, :].to_broadcast([P, 2, 2 * P]),
                                            ALU.mult).then_inc(ab_done, 1)
                    dve.wait_ge(ab_done, n.of("RO") * TT + (t + 1))
                    a4 = rot_a.rearrange("p (h i two) -> p h i two", h=2, two=2)
                    b4 = rot_b.rearrange("p (h i two) -> p h i two", h=2, two=2)
                    o4 = rot[:, t, :].rearrange("p (h two i) -> p h two i", h=2, two=2)
                    nc.vector.tensor_tensor(o4[:, :, 0, :], a4[:, :, :, 0], b4[:, :, :, 1], ALU.subtract)
                    nc.vector.tensor_tensor(o4[:, :, 1, :], b4[:, :, :, 0], a4[:, :, :, 1],
                                            ALU.add).then_inc(rot_done, 1)

            def step(what, r):
                name, hd = what
                if name == "probs":
                    dve.wait_ge(score_done, n.of("SC") + 1)
                    table = decay[:, bass.ds(r * GROUP_HEADS + hd, 1), :].rearrange("p h t -> p (h t)")
                    nc.vector.tensor_tensor(probs[:, 0:S], score_ps[:, 0:S], table, ALU.mult)
                    nc.vector.tensor_tensor(probs[:, S:S + P], score_ps[:, S:S + P], table[:, 0:P],
                                            ALU.mult).then_inc(prob_done, 1)
                    n.add(SC=1)
                elif name == "norm":
                    for t in range(TT):
                        dve.wait_ge(evac, n.of("E") * TT + (t + 1))
                        nc.vector.bn_stats(y_stats[:, t, :], ybuf[:, t, :]).then_inc(bn_done, 1)
                    for t in range(TT):
                        dve.wait_ge(ret_in, 48)
                        dve.wait_ge(bn_done, n.of("Y") * TT + (t + 1))
                        nc.vector.bn_aggr(y_mv[:, t, :], y_stats[:, t, :]).then_inc(mv_done, 1)
                    dve.wait_ge(mv_done, (n.of("Y") + 1) * TT)
                    nc.vector.tensor_scalar(y_var[:], y_mv[:, :, 1], EPS, None, ALU.add).then_inc(var_done, 1)
                    for t in range(TT):
                        nc.vector.scalar_tensor_tensor(out=ybuf[:, t, :], in0=ybuf[:, t, :], scalar=y_mv[:, t, 0:1],
                                                       in1=ev[:, 0, t, :], op0=ALU.subtract,
                                                       op1=ALU.mult).then_inc(z_mul, 1)
                    n.add(E=1, Y=1)
                else:
                    for b in range(2):
                        lower_T(4 * hd + 2 * b, b)

            def retention():
                gains()
                for f in range(KT // 2):
                    split_h(f)
                dve.wait_ge(gate_in, 16 * n.of("GB"))
                dve.wait_ge(ret_in, 48)
                with dve.Fori(0, 2) as r:
                    n.enter(r, R_ROUND)
                    for i, kind in enumerate(R_KINDS):
                        hooks = {s: [lambda w=w: step(w, r) for w in ws] for s, ws in DVE_STEPS.get(i, {}).items()}
                        if i in (1, 7):
                            hooks.setdefault(4, []).append(lambda: n.add(TB=2))
                        if i in (2, 8):
                            hooks.setdefault(3, []).append(lambda: n.add(TB=2))
                        if i == R_UNITS - 1:
                            hooks[2] = [lambda: take_rows(0, 4)]
                        steps(hooks, sum(ADA_RET[:i]), ADA_RET[i], LEAD - (i == R_UNITS - 1))
                        if kind in ("q", "k"):
                            rotate(i % 2, i)
                        elif kind == "m2":
                            add_block(i % 2, i - 12)
                            if i == R_UNITS - 1:
                                lo(LEAD - 1, 1)
                        n.unit(kind)
                    n.add(SB=3)
                    n.add(CS=1)
                    take_column(bass.ds(r + 6, 1))
                n.leave(2)

            def between():
                mean_square()
                diagonals()

            mlp(0)
            between()
            retention()
            between()
            mlp(1)
            mean_square()
            dve.wait_ge(rstd_done, 5)
            dve.wait_ge(y_gained, 4 * TT)
            for half in range(2):
                cols = slice(half * AW, (half + 1) * AW)
                nc.vector.tensor_scalar(x[:, 0, cols], y_end[:, 0, cols], rstd[:, 0:1], None,
                                        ALU.mult).then_inc(o_ready, 1)

        @block.gpsimd
        def _(pool):
            n = Count()

            def inverse_root():
                pool.wait_ge(ms_done, n.n["NO"] + 1)
                nc.gpsimd.tensor_tensor(rstd[:], meansq[:], minus_half[:], ALU.pow).then_inc(rstd_done, 1)
                n.add(NO=1)

            nc.gpsimd.memset(col_rows[:], 0.0)
            nc.gpsimd.memset(rows[:], 0.0).then_inc(rows_zero, 1)
            nc.gpsimd.memset(ones[:], 1.0).then_inc(ones_set, 1)
            nc.gpsimd.memset(minus_half[:], -0.5).then_inc(half_set, 1)
            pool.wait_ge(half_set, 1)
            for _ in range(3):
                inverse_root()
            for hd in range(HEADS):
                pool.wait_ge(var_done, hd + 1)
                nc.gpsimd.tensor_tensor(y_rstd[:], y_var[:], minus_half[:], ALU.pow).then_inc(z_rstd, 1)
            for _ in range(2):
                inverse_root()


_INS = ["x", "c", "ada_w", "ada_b", "norm_g", "pool_w", "pool_scale", "ret_w_in", "ret_w_out", "mlp_w1", "mlp_w2",
        "final_g"]


def tables():
    ident = np.eye(P, dtype=np.float32)
    inv = np.float32(10000.0) ** (-np.arange(0, 2 * P, 2, dtype=np.float32) / np.float32(2 * P))
    ang = (np.arange(S, dtype=np.float32)[:, None] * inv[None, :]).astype(np.float64)

    def by_token(a):
        return np.ascontiguousarray(np.repeat(a, 2, axis=1).reshape(TT, P, 2 * P).transpose(1, 0, 2).astype(np.float32))

    log_g = np.log(1.0 - 2.0 ** (-5.0 - np.arange(HEADS)))
    j = np.arange(P, dtype=np.float64)
    diff = j[None, :] - j[:, None]
    decay = np.zeros((P, HEADS, S))
    for h in range(HEADS):
        decay[:, h, 0:P] = np.where(diff >= 0, np.exp(np.maximum(diff, 0.0) * log_g[h]), 0.0)
        decay[:, h, P:S] = np.exp((j[None, :] + 1.0) * log_g[h]) * np.exp((P - 1.0 - j[:, None]) * log_g[h])
    decay *= (2 * P) ** -0.5
    rcount = np.broadcast_to(1.0 / np.arange(1, 17), (P, 4, 16))
    return dict(ident=ident, cos=by_token(np.cos(ang)), sin=by_token(np.sin(ang)),
                decay=decay.astype(np.float32), rcount=np.ascontiguousarray(rcount.astype(np.float32)))


def kernel(**inputs):
    import concourse.bacc as _bacc
    from concourse.bass_utils import run_bass_kernel_spmd as _run

    nc = _bacc.Bacc("TRN2", target_bir_lowering=False, num_devices=1,
                     dynamic_dma_scratch_size=8192)
    arrays, args = {}, []
    data = {name: np.ascontiguousarray(inputs[name]) for name in _INS}
    data.update(tables())
    for name, a in data.items():
        arrays[f"in_{name}"] = a
        args.append(nc.dram_tensor(f"in_{name}", a.shape, mybir.dt.from_np(a.dtype), kind="ExternalInput").ap())
    out = nc.dram_tensor("out_0", (1, S, D), F32, kind="ExternalOutput").ap()
    program(nc, *args, out)
    r = _run(nc, [arrays], core_ids=[0])
    return r.results[0]["out_0"]
```
